# Optimizing a Trainium2 kernel written in Bass

```python
import jax, jax.numpy as jnp
from jax import lax
import numpy as np

D_MODEL = 1024
BATCH = 1
SEQ = 512
DEPTH = 1

CHUNK = 128
N_SGU_GROUPS = 8
SGU_WIDTH = D_MODEL
SGU_GROUP_DIM = SGU_WIDTH // N_SGU_GROUPS
N_HEADS = 8
HEAD_DIM = 128
ATTN_WIDTH = N_HEADS * HEAD_DIM
Q_BLOCK = 128
D_FF = -(-8 * D_MODEL // (3 * 256)) * 256
EPS = 1e-6

_IN_SIZES = (SGU_WIDTH, SGU_WIDTH, ATTN_WIDTH, ATTN_WIDTH, ATTN_WIDTH, D_MODEL, D_MODEL, N_HEADS)
IN_WIDTH = sum(_IN_SIZES)
IN_SPLITS = tuple(int(s) for s in np.cumsum(_IN_SIZES)[:-1])


def rmsnorm(x, g):
    xf = x.astype(jnp.float32)
    r = lax.rsqrt(jnp.mean(xf * xf, axis=-1, keepdims=True) + EPS)
    return (xf * r * g.astype(jnp.float32)).astype(x.dtype)

def layernorm(x, g):
    xf = x.astype(jnp.float32)
    mu = jnp.mean(xf, axis=-1, keepdims=True)
    xc = xf - mu
    r = lax.rsqrt(jnp.mean(xc * xc, axis=-1, keepdims=True) + EPS)
    return (xc * r * g.astype(jnp.float32)).astype(x.dtype)

def spatial_gating(u, v, w_s, b_s, g_v):
    bsz, seq = v.shape[0], v.shape[1]
    v = layernorm(v, g_v)
    vc = v.reshape(bsz, seq // CHUNK, CHUNK, N_SGU_GROUPS, SGU_GROUP_DIM)
    causal = jnp.tril(jnp.ones((CHUNK, CHUNK), dtype=bool))
    w = jnp.where(causal[None], w_s, jnp.zeros_like(w_s))
    mixed = jnp.einsum('gts,bcsgd->bctgd', w, vc) + b_s.T[None, None, :, :, None]
    return u * mixed.reshape(bsz, seq, SGU_WIDTH)

def forgetting_attention(q, k, v, f_logit, b_f):
    bsz, seq = q.shape[0], q.shape[1]

    def heads(t):
        return t.reshape(bsz, seq, N_HEADS, HEAD_DIM).transpose(0, 2, 1, 3)

    q = heads(q) * (HEAD_DIM ** -0.5)
    k = heads(k)
    v = heads(v)
    log_f = jax.nn.log_sigmoid((f_logit + b_f).astype(jnp.float32))
    c = jnp.cumsum(log_f, axis=1).transpose(0, 2, 1)
    k_pos = jnp.arange(seq)

    def block(i):
        start = i * Q_BLOCK
        qi = lax.dynamic_slice_in_dim(q, start, Q_BLOCK, axis=2)
        ci = lax.dynamic_slice_in_dim(c, start, Q_BLOCK, axis=2)
        s = jnp.einsum('bhqd,bhkd->bhqk', qi, k).astype(jnp.float32)
        s = s + ci[..., None] - c[:, :, None, :]
        q_pos = start + jnp.arange(Q_BLOCK)
        s = jnp.where(k_pos[None, :] <= q_pos[:, None], s, -jnp.inf)
        p = jax.nn.softmax(s, axis=-1).astype(v.dtype)
        return jnp.einsum('bhqk,bhkd->bhqd', p, v)

    out = lax.map(block, jnp.arange(seq // Q_BLOCK))
    return out.transpose(1, 0, 3, 2, 4).reshape(bsz, seq, ATTN_WIDTH)

def swiglu(h, w_gate, w_up, w_down):
    return (jax.nn.silu(h @ w_gate) * (h @ w_up)) @ w_down

def first_inputs(seed: int = 0) -> dict:
    key = jax.random.key(seed)
    ks = jax.random.split(key, 15)
    f32 = jnp.float32

    def nrm(k, shape, scale):
        return jax.random.normal(k, shape, f32) * scale

    def gain(k, shape):
        return 1.0 + 0.1 * jax.random.normal(k, shape, f32)

    x = jax.random.normal(ks[0], (BATCH, SEQ, D_MODEL), f32)
    mix_pre_g = gain(ks[1], (DEPTH, D_MODEL))
    w_in = nrm(ks[2], (DEPTH, D_MODEL, IN_WIDTH), D_MODEL ** -0.5)
    b_forget = jnp.linspace(1.0, 6.0, N_HEADS, dtype=f32)[None, :] + 0.1 * jax.random.normal(ks[3], (DEPTH, N_HEADS), f32)
    sgu_norm_g = gain(ks[4], (DEPTH, SGU_WIDTH))
    w_spatial = nrm(ks[5], (DEPTH, N_SGU_GROUPS, CHUNK, CHUNK), CHUNK ** -0.5)
    b_spatial = 1.0 + 0.1 * jax.random.normal(ks[6], (DEPTH, N_SGU_GROUPS, CHUNK), f32)
    w_out = nrm(ks[7], (DEPTH, D_MODEL, D_MODEL), D_MODEL ** -0.5)
    mix_post_g = gain(ks[8], (DEPTH, D_MODEL))
    ffn_pre_g = gain(ks[9], (DEPTH, D_MODEL))
    w_gate = nrm(ks[10], (DEPTH, D_MODEL, D_FF), D_MODEL ** -0.5)
    w_up = nrm(ks[11], (DEPTH, D_MODEL, D_FF), D_MODEL ** -0.5)
    w_down = nrm(ks[12], (DEPTH, D_FF, D_MODEL), D_FF ** -0.5)
    ffn_post_g = gain(ks[13], (DEPTH, D_MODEL))
    return {"x": x, "mix_pre_g": mix_pre_g, "w_in": w_in, "b_forget": b_forget,
            "sgu_norm_g": sgu_norm_g, "w_spatial": w_spatial, "b_spatial": b_spatial,
            "w_out": w_out, "mix_post_g": mix_post_g, "ffn_pre_g": ffn_pre_g,
            "w_gate": w_gate, "w_up": w_up, "w_down": w_down, "ffn_post_g": ffn_post_g}

def first_block(x, mix_pre_g, w_in, b_forget, sgu_norm_g, w_spatial, b_spatial, w_out,
              mix_post_g, ffn_pre_g, w_gate, w_up, w_down, ffn_post_g):
    for l in range(DEPTH):
        h = rmsnorm(x, mix_pre_g[l])
        proj = h @ w_in[l]
        u, v_s, q, k, v_a, g_a, g_b, f_logit = jnp.split(proj, IN_SPLITS, axis=-1)
        y_a = spatial_gating(jax.nn.gelu(u), jax.nn.gelu(v_s), w_spatial[l], b_spatial[l], sgu_norm_g[l])
        y_b = forgetting_attention(q, k, v_a, f_logit, b_forget[l])
        merged = jax.nn.sigmoid(g_a) * y_a + jax.nn.sigmoid(g_b) * y_b
        x = x + rmsnorm(merged @ w_out[l], mix_post_g[l])
        h = rmsnorm(x, ffn_pre_g[l])
        x = x + rmsnorm(swiglu(h, w_gate[l], w_up[l], w_down[l]), ffn_post_g[l])
    return x


SC_WIDTH = D_MODEL // 4
SC_GROUPS = 4
SC_KERNEL = 3
SB_HEAD_DIM = 64
SB_HEADS = (D_MODEL // 4) // SB_HEAD_DIM
SB_WIDTH = SB_HEADS * SB_HEAD_DIM
SB_BLOCK = 128
SSM_INNER = D_MODEL // 2
SSM_HEAD_DIM = 64
SSM_HEADS = SSM_INNER // SSM_HEAD_DIM
SSM_GROUPS = 2
SSM_STATE = 64
SSM_CONV = 4
SSM_CHUNK = 256
SSM_CONV_DIM = SSM_INNER + 2 * SSM_GROUPS * SSM_STATE
N_BRANCH = 3
FFN_HIDDEN = -(-8 * D_MODEL // (3 * 256)) * 256
NORM_EPS = 1e-6
N_MOD = 6
PROJ_SIZES = (SC_WIDTH, SC_WIDTH, SC_WIDTH,
              SB_WIDTH, SB_WIDTH, SB_WIDTH,
              SSM_INNER, SSM_CONV_DIM, SSM_HEADS,
              D_MODEL, D_MODEL, D_MODEL)
IN_PROJ = sum(PROJ_SIZES)


def rms_norm(x, g):
    x32 = x.astype(jnp.float32)
    y = x32 * lax.rsqrt(jnp.mean(x32 * x32, axis=-1, keepdims=True) + NORM_EPS)
    return (y * g.astype(jnp.float32)).astype(x.dtype)

def causal_depthwise_conv(x, w):
    k = w.shape[0]
    return lax.conv_general_dilated(
        x, w[:, None, :].astype(x.dtype), window_strides=(1,), padding=[(k - 1, 0)],
        dimension_numbers=("NWC", "WIO", "NWC"), feature_group_count=x.shape[-1])

def split_columns(p):
    offsets = [int(o) for o in np.cumsum(PROJ_SIZES)[:-1]]
    return jnp.split(p, offsets, axis=-1)

def short_conv_mixer(b_gate, c_gate, xa, w_conv):
    return b_gate * causal_depthwise_conv(c_gate * xa, w_conv)

def stick_breaking_attention(q, k, v):
    bsz, seq, heads, dh = q.shape
    n_blk = seq // SB_BLOCK
    scale = dh ** -0.5
    qh = q.transpose(0, 2, 1, 3)
    kh = k.transpose(0, 2, 1, 3)
    vh = v.transpose(0, 2, 1, 3)
    strict = jnp.tril(jnp.ones((SB_BLOCK, SB_BLOCK), jnp.float32), -1)
    outs = []
    for i in range(n_blk):
        start, end = i * SB_BLOCK, (i + 1) * SB_BLOCK
        z = jnp.einsum("bhqd,bhkd->bhqk", qh[:, :, start:end], kh[:, :, :end],
                       preferred_element_type=jnp.float32) * scale
        mask = jnp.arange(end)[None, :] < (start + jnp.arange(SB_BLOCK))[:, None]
        log_keep = jnp.where(mask, jax.nn.log_sigmoid(-z), 0.0)
        lk = log_keep.reshape(bsz, heads, SB_BLOCK, i + 1, SB_BLOCK)
        within = jnp.einsum("bhqcj,js->bhqcs", lk, strict)
        blk_tot = jnp.sum(lk, axis=-1)
        later = lax.cumsum(blk_tot, axis=3, reverse=True) - blk_tot
        log_rest = (within + later[..., None]).reshape(bsz, heads, SB_BLOCK, end)
        att = jnp.exp(jnp.where(mask, z + log_keep + log_rest, -jnp.inf))
        outs.append(jnp.einsum("bhqk,bhkd->bhqd", att.astype(vh.dtype), vh[:, :, :end]))
    out = jnp.concatenate(outs, axis=2)
    return out.transpose(0, 2, 1, 3).reshape(bsz, seq, heads * dh)

def segsum_exp(a_cs):
    l = a_cs.shape[-1]
    mask = jnp.tril(jnp.ones((l, l), dtype=bool))
    diff = a_cs[..., :, None] - a_cs[..., None, :]
    return jnp.exp(jnp.where(mask, diff, -jnp.inf))

def ssd_scan(xh, dt, a_neg, bm, cm):
    bsz, seq, heads, hd = xh.shape
    reps = heads // bm.shape[2]
    bh = jnp.repeat(bm, reps, axis=2)
    ch = jnp.repeat(cm, reps, axis=2)
    xdt = xh * dt[..., None]
    a = dt * a_neg
    pad = (-seq) % SSM_CHUNK
    if pad:
        pw = ((0, 0), (0, pad), (0, 0), (0, 0))
        xdt, bh, ch = jnp.pad(xdt, pw), jnp.pad(bh, pw), jnp.pad(ch, pw)
        a = jnp.pad(a, ((0, 0), (0, pad), (0, 0)))
    n_c = (seq + pad) // SSM_CHUNK
    xc = xdt.reshape(bsz, n_c, SSM_CHUNK, heads, hd)
    bc = bh.reshape(bsz, n_c, SSM_CHUNK, heads, -1)
    cc = ch.reshape(bsz, n_c, SSM_CHUNK, heads, -1)
    a_cs = jnp.cumsum(a.reshape(bsz, n_c, SSM_CHUNK, heads), axis=2)
    decay_in = segsum_exp(a_cs.transpose(0, 1, 3, 2))
    scores = jnp.einsum("bclhn,bcshn->bchls", cc, bc) * decay_in
    y_diag = jnp.einsum("bchls,bcshp->bclhp", scores, xc)
    decay_to_end = jnp.exp(a_cs[:, :, -1:, :] - a_cs)
    chunk_states = jnp.einsum("bclhn,bclhp->bchpn", bc * decay_to_end[..., None], xc)
    chunk_decay = jnp.exp(a_cs[:, :, -1, :])

    def step(state, inp):
        s_c, d_c = inp
        return state * d_c[..., None, None] + s_c, state

    init = jnp.zeros((bsz, heads, hd, bc.shape[-1]), jnp.float32)
    _, prev = lax.scan(step, init, (chunk_states.transpose(1, 0, 2, 3, 4),
                                    chunk_decay.transpose(1, 0, 2)))
    prev = prev.transpose(1, 0, 2, 3, 4)
    y_off = jnp.einsum("bclhn,bchpn->bclhp", cc, prev) * jnp.exp(a_cs)[..., None]
    return (y_diag + y_off).reshape(bsz, seq + pad, heads, hd)[:, :seq]

def mamba2_mixer(z, xbc, dt_raw, conv_w, conv_b, dt_bias, a_log, d_skip, norm_w):
    xbc = jax.nn.silu(causal_depthwise_conv(xbc, conv_w) + conv_b)
    xs, bm, cm = jnp.split(xbc, [SSM_INNER, SSM_INNER + SSM_GROUPS * SSM_STATE], axis=-1)
    bsz, seq, _ = xs.shape
    xh = xs.reshape(bsz, seq, SSM_HEADS, SSM_HEAD_DIM).astype(jnp.float32)
    bm = bm.reshape(bsz, seq, SSM_GROUPS, SSM_STATE).astype(jnp.float32)
    cm = cm.reshape(bsz, seq, SSM_GROUPS, SSM_STATE).astype(jnp.float32)
    dt = jax.nn.softplus(dt_raw.astype(jnp.float32) + dt_bias.astype(jnp.float32))
    a_neg = -jnp.exp(a_log.astype(jnp.float32))
    y = ssd_scan(xh, dt, a_neg, bm, cm) + xh * d_skip.astype(jnp.float32)[:, None]
    y = y.reshape(bsz, seq, SSM_INNER) * jax.nn.silu(z.astype(jnp.float32))
    yg = y.reshape(bsz, seq, SSM_GROUPS, SSM_INNER // SSM_GROUPS)
    yg = yg * lax.rsqrt(jnp.mean(yg * yg, axis=-1, keepdims=True) + NORM_EPS)
    return (yg.reshape(bsz, seq, SSM_INNER) * norm_w.astype(jnp.float32)).astype(z.dtype)

def hybrid_layer(x, c, mod_w, mod_b, g_pre_mix, g_post_mix, g_pre_ffn, g_post_ffn,
                 w_in, sc_conv_w, ssm_conv_w, ssm_conv_b, ssm_dt_bias, ssm_a_log, ssm_d,
                 ssm_norm_w, w_sc_out, w_sb_out, w_ssm_out, w_o, w_ffn_in, w_ffn_out):
    bsz, seq, _ = x.shape
    mod = jax.nn.silu(c) @ mod_w + mod_b
    shift1, scale1, gate1, shift2, scale2, gate2 = [m[:, None, :] for m in jnp.split(mod, N_MOD, axis=-1)]

    h = rms_norm(x, g_pre_mix) * (1 + scale1) + shift1
    (sc_b, sc_c, sc_x, q, k, v, z, xbc, dt_raw,
     gl_a, gl_b, gl_c) = split_columns(h @ w_in)
    y_a = short_conv_mixer(sc_b, sc_c, sc_x, sc_conv_w) @ w_sc_out
    y_b = stick_breaking_attention(
        q.reshape(bsz, seq, SB_HEADS, SB_HEAD_DIM),
        k.reshape(bsz, seq, SB_HEADS, SB_HEAD_DIM),
        v.reshape(bsz, seq, SB_HEADS, SB_HEAD_DIM)) @ w_sb_out
    y_c = mamba2_mixer(z, xbc, dt_raw, ssm_conv_w, ssm_conv_b, ssm_dt_bias, ssm_a_log,
                       ssm_d, ssm_norm_w) @ w_ssm_out
    merged = (jax.nn.sigmoid(gl_a) * y_a + jax.nn.sigmoid(gl_b) * y_b
              + jax.nn.sigmoid(gl_c) * y_c)
    mix_out = merged @ w_o
    x = x + (gate1 * rms_norm(mix_out, g_post_mix)).astype(x.dtype)

    h2 = rms_norm(x, g_pre_ffn) * (1 + scale2) + shift2
    gt, up = jnp.split(h2 @ w_ffn_in, 2, axis=-1)
    f = (jax.nn.silu(gt) * up) @ w_ffn_out
    x = x + (gate2 * rms_norm(f, g_post_ffn)).astype(x.dtype)
    return x

def second_inputs(seed: int = 0) -> dict:
    key = jax.random.key(seed)
    ks = jax.random.split(key, 24)
    f32 = jnp.float32

    def nrm(k, shape, fan_in):
        return jax.random.normal(k, shape, f32) * (fan_in ** -0.5)

    def gain(k, shape):
        return 1.0 + 0.05 * jax.random.normal(k, shape, f32)

    dt0 = jnp.exp(jax.random.uniform(ks[14], (DEPTH, SSM_HEADS), f32,
                                     jnp.log(1e-3), jnp.log(1e-1)))
    return {
        "x": jax.random.normal(ks[0], (BATCH, SEQ, D_MODEL), f32),
        "c": jax.random.normal(ks[1], (BATCH, D_MODEL), f32),
        "mod_w": nrm(ks[2], (DEPTH, D_MODEL, N_MOD * D_MODEL), D_MODEL),
        "mod_b": 0.02 * jax.random.normal(ks[3], (DEPTH, N_MOD * D_MODEL), f32),
        "g_pre_mix": gain(ks[4], (DEPTH, D_MODEL)),
        "g_post_mix": gain(ks[5], (DEPTH, D_MODEL)),
        "g_pre_ffn": gain(ks[6], (DEPTH, D_MODEL)),
        "g_post_ffn": gain(ks[7], (DEPTH, D_MODEL)),
        "w_in": nrm(ks[8], (DEPTH, D_MODEL, IN_PROJ), D_MODEL),
        "sc_conv_w": nrm(ks[9], (DEPTH, SC_KERNEL, SC_WIDTH), SC_KERNEL),
        "ssm_conv_w": nrm(ks[10], (DEPTH, SSM_CONV, SSM_CONV_DIM), SSM_CONV),
        "ssm_conv_b": 0.02 * jax.random.normal(ks[11], (DEPTH, SSM_CONV_DIM), f32),
        "ssm_dt_bias": dt0 + jnp.log(-jnp.expm1(-dt0)),
        "ssm_a_log": jnp.log(jax.random.uniform(ks[12], (DEPTH, SSM_HEADS), f32, 1.0, 16.0)),
        "ssm_d": 1.0 + 0.1 * jax.random.normal(ks[13], (DEPTH, SSM_HEADS), f32),
        "ssm_norm_w": gain(ks[15], (DEPTH, SSM_INNER)),
        "w_sc_out": nrm(ks[16], (DEPTH, SC_WIDTH, D_MODEL), SC_WIDTH),
        "w_sb_out": nrm(ks[17], (DEPTH, SB_WIDTH, D_MODEL), SB_WIDTH),
        "w_ssm_out": nrm(ks[18], (DEPTH, SSM_INNER, D_MODEL), SSM_INNER),
        "w_o": nrm(ks[19], (DEPTH, D_MODEL, D_MODEL), D_MODEL),
        "w_ffn_in": nrm(ks[20], (DEPTH, D_MODEL, 2 * FFN_HIDDEN), D_MODEL),
        "w_ffn_out": nrm(ks[21], (DEPTH, FFN_HIDDEN, D_MODEL), FFN_HIDDEN),
    }

def second_block(x, c, mod_w, mod_b, g_pre_mix, g_post_mix, g_pre_ffn, g_post_ffn, w_in,
              sc_conv_w, ssm_conv_w, ssm_conv_b, ssm_dt_bias, ssm_a_log, ssm_d, ssm_norm_w,
              w_sc_out, w_sb_out, w_ssm_out, w_o, w_ffn_in, w_ffn_out):
    for l in range(DEPTH):
        x = hybrid_layer(x, c, mod_w[l], mod_b[l], g_pre_mix[l], g_post_mix[l],
                         g_pre_ffn[l], g_post_ffn[l], w_in[l], sc_conv_w[l], ssm_conv_w[l],
                         ssm_conv_b[l], ssm_dt_bias[l], ssm_a_log[l], ssm_d[l], ssm_norm_w[l],
                         w_sc_out[l], w_sb_out[l], w_ssm_out[l], w_o[l], w_ffn_in[l],
                         w_ffn_out[l])
    return x


def setup_inputs(seed=0):
    out = dict(first_inputs(seed))
    for name, value in second_inputs(seed + 1).items():
        if name != "x":
            out[name + "_2"] = value
    return out


def reference(
    x, mix_pre_g, w_in, b_forget, sgu_norm_g, w_spatial, b_spatial, w_out, mix_post_g,
    ffn_pre_g, w_gate, w_up, w_down, ffn_post_g, c_2, mod_w_2, mod_b_2, g_pre_mix_2,
    g_post_mix_2, g_pre_ffn_2, g_post_ffn_2, w_in_2, sc_conv_w_2, ssm_conv_w_2, ssm_conv_b_2,
    ssm_dt_bias_2, ssm_a_log_2, ssm_d_2, ssm_norm_w_2, w_sc_out_2, w_sb_out_2, w_ssm_out_2,
    w_o_2, w_ffn_in_2, w_ffn_out_2,
):
    x = first_block(
        x, mix_pre_g, w_in, b_forget, sgu_norm_g, w_spatial, b_spatial, w_out, mix_post_g,
        ffn_pre_g, w_gate, w_up, w_down, ffn_post_g,
    )
    return second_block(
        x, c_2, mod_w_2, mod_b_2, g_pre_mix_2, g_post_mix_2, g_pre_ffn_2, g_post_ffn_2, w_in_2,
        sc_conv_w_2, ssm_conv_w_2, ssm_conv_b_2, ssm_dt_bias_2, ssm_a_log_2, ssm_d_2,
        ssm_norm_w_2, w_sc_out_2, w_sb_out_2, w_ssm_out_2, w_o_2, w_ffn_in_2, w_ffn_out_2,
    )


_drawn_inputs = setup_inputs


def setup_inputs(seed=0):
    import zlib

    import numpy as np

    out = dict(_drawn_inputs(seed))
    spreads = {}
    factors = {'g_post_mix_2': 3.342,
     'g_pre_ffn_2': 2.841,
     'g_post_ffn_2': 3.59,
     'ssm_conv_b_2': 8.0,
     'ssm_a_log_2': 4.113,
     'ssm_d_2': 7.059,
     'ssm_norm_w_2': 8.0}
    for name, (base, spread) in spreads.items():
        noise = np.random.default_rng([zlib.crc32(name.encode()), seed]).standard_normal(out[name].shape)
        drawn = base * np.exp(spread * noise) if base else spread * noise
        out[name] = __import__('jax').numpy.asarray(drawn.astype(out[name].dtype))
    for name, factor in factors.items():
        out[name] = (out[name] * factor).astype(out[name].dtype)
    return out
```

```python
from contextlib import ExitStack

import numpy as np
import concourse.bass as bass
from concourse import mybir

F32 = mybir.dt.float32
F32R = mybir.dt.float32r
ALU = mybir.AluOpType
ACT = mybir.ActivationFunctionType
AX_X = mybir.AxisListType.X

P = 128
TOK = 512
NT = TOK // P
D = 1024
KD = D // P
FF = 2816
KF = FF // P
HEADS = 8
EPS = 1e-6
MASKED = -1e30
KB = 1024

U_COL, VS_COL, Q_COL, K_COL, VA_COL, GA_COL, GB_COL, F_COL = (D * n for n in range(8))
SC_COL, SBQ_COL, SBV_COL, Z_COL, XBC_COL, DT_COL, GATE_COL = 0, 768, 1280, 1536, 2048, 2816, 2824
SB_HEADS = 4
SSM_HD = 64
CONV_K, SHORT_K = 4, 3
PAD = CONV_K

STREAM = [
    ("q", "F", 4), ("k", "F", 4), ("va", "T", 4), ("gates", "F", 8), ("vs", "T", 4), ("u", "F", 4),
    ("out", "T", 4), ("up", "F", 22), ("down", "D", 12),
    ("sbqk", "F", 2), ("sbv", "V", 1), ("xbc", "F", 3), ("z", "F", 2), ("sc", "F", 3),
    ("merge", "B", 16), ("out2", "T", 4), ("up2", "F", 22), ("down2", "D", 12),
]


def lay_out_stream():
    units, first = [], {}
    raw = [0, 0]
    full = mid = half = 0
    for stage, kind, count in STREAM:
        first[stage] = len(units)
        for n in range(count):
            u = {"n": len(units), "slot": len(units) % 2, "round": half // 2, "half": half % 2, "kt": 4}
            raw[u["slot"]] += 48 if (kind == "B" and n % 4 == 3) else 32
            u["raw"] = raw[u["slot"]]
            banks = {"F": 2, "B": 2, "V": 4}.get(kind, 0)
            if kind == "T":
                banks = 4 if n % 2 else 0
            if kind == "D":
                banks = 4 if n % 6 == 5 else 0
                u["kt"] = 2 if n % 6 == 5 else 4
            full += banks
            half += banks // 2
            mid += banks == 0
            u["used"] = ("full", full) if banks else ("mid", mid)
            u["full"] = full - banks
            units.append(u)
    return units, first


UNITS, FIRST = lay_out_stream()


class Pace:

    def __init__(self, turn=None, units=0, rounds=0, mids=0, raw=(0, 0)):
        self.turn, self.units, self.rounds, self.mids, self.raw = turn, units, rounds, mids, raw

    def by(self, per_turn):
        return 0 if self.turn is None else self.turn * per_turn


STILL = Pace()


def pair_pace(turn):
    return Pace(turn, units=2, rounds=1, raw=(32, 32))


def chunk_pace(turn):
    return Pace(turn, units=2, rounds=1, mids=1, raw=(32, 32))


def down_pace(turn):
    return Pace(turn, units=6, rounds=1, mids=5, raw=(96, 96))


def merge_pace(turn):
    slot_of_branch = (FIRST["merge"] + 3) % 2
    return Pace(turn, units=4, rounds=2, raw=(80, 64) if slot_of_branch == 0 else (64, 80))


def build(nc, a, out):
    with ExitStack() as ctx:
        base = 16512

        def at(name, kb, shape, dt=F32):
            return nc.alloc_sbuf_tensor_at(name, shape, dt, offset=base + int(kb * KB))

        def sem(name):
            return ctx.enter_context(nc.semaphore(name))

        raw = [at(f"raw{s}", 8 * s, [P, 2048]) for s in range(2)]
        w_hi = [at(f"w_hi{s}", 16 + 8 * s, [P, 2048], F32R) for s in range(2)]
        w_lo = [at(f"w_lo{s}", 32 + 8 * s, [P, 2048], F32R) for s in range(2)]
        h_hi = at("h_hi", 48, [P, KD, TOK], F32R)
        h_lo = at("h_lo", 64, [P, KD, TOK], F32R)
        y_down = at("y_down", 48, [P, NT, D])
        x_res = at("x_res", 80, [P, NT, D])
        v_att = at("v_att", 80, [P, NT, D])
        mrg_hi = at("mrg_hi", 80, [P, KD, TOK], F32R)
        A = 96
        x_in = at("x_in", A + 32, [P, NT, D])
        xn_1 = at("xn_1", A + 0, [P, NT, D])
        xn_2 = at("xn_2", A + 16, [P, NT, D])
        h_tmp = at("h_tmp", A + 48, [P, 2, TOK])
        q_t = at("q_t", A + 0, [P, HEADS, TOK])
        k_t = at("k_t", A + 16, [P, HEADS, TOK])
        v_sgu = at("v_sgu", A + 16, [P, NT, D])
        gates = at("gate_a", A + 32, [P, 2 * KD, TOK])
        u_act = at("u_act", A + 48, [P, 2, TOK])
        m_tmp = at("m_tmp", A + 52, [P, 2, TOK])
        prob = at("prob", A + 64, [P, 2, TOK])
        prob_t = at("prob_t", A + 68, [P, 2, TOK])
        c_rows = at("c_rows", A + 72, [64, TOK], F32R)
        w_sp = at("w_sp", A + 76, [P, HEADS, P])
        mrg_lo = at("mrg_lo", A + 64, [P, KD, TOK], F32R)
        w_sp_t = at("w_sp_t", A + 80, [P, HEADS, P])
        b_sp = at("b_sp", A + 84, [P, HEADS, P])
        y_out = at("y_out", A + 0, [P, NT, D])
        act_hi = at("act_hi", A + 0, [P, KF, TOK], F32R)
        act_lo = at("act_lo", A + 44, [P, KF, TOK], F32R)
        sb_hi = at("sb_hi", A + 0, [P, 2, TOK], F32R)
        sb_lo = at("sb_lo", A + 4, [P, 2, TOK], F32R)
        sc_hi = at("sc_hi", A + 8, [P, 2, TOK], F32R)
        sc_lo = at("sc_lo", A + 12, [P, 2, TOK], F32R)
        ssm_hi = at("ssm_hi", A + 16, [P, 4, TOK], F32R)
        ssm_lo = at("ssm_lo", A + 24, [P, 4, TOK], F32R)
        qk2 = at("qk2", A + 16, [P, 4, TOK])
        v2 = at("v2", A + 24, [P, NT, 256])
        sc_raw = at("sc_raw", A + 16, [P, 6, TOK + PAD])
        z_t = at("z_t", A + 32, [P, 4, TOK])
        y_ssm = at("y_ssm", A + 40, [P, 4, TOK])
        sp_all = at("sp_all", A + 40, [P, 1280])
        xs_t = at("xs_t", A + 48, [P, 6, TOK])
        sp_tmp = at("sp_tmp", A + 60, [P, 2, TOK])
        att = at("att", A + 64, [P, 2, TOK])
        xdt = at("xdt", A + 60, [P, NT, TOK])
        xbc_raw = at("xbc_raw", A + 68, [P, 6, TOK + PAD])
        cb = at("cb", A + 68, [P, 2, 1280])
        decay = at("decay", A + 78, [P, 2, TOK])
        g_ssd = at("g_ssd", A + 82, [P, 2, TOK])
        a_rows = at("a_rows", A + 86, [64, TOK], F32R)
        rr_diag = at("rr_diag", A + 68, [P, 2 * NT, P])
        m2_hi = at("m2_hi", A + 40, [P, KD, TOK], F32R)
        m2_lo = at("m2_lo", A + 56, [P, KD, TOK], F32R)
        sig = at("sig", A + 72, [P, 6, TOK])
        m2_tmp = at("m2_tmp", A + 84, [P, 2, TOK])
        M = 184
        ident_r = at("ident", M, [P, P], F32R)
        ident = ident_r[:].bitcast(F32)
        ones = at("ones", M + 0.5, [P, P])
        mask_qk = at("mask_qk", M + 1, [P, P], F32R)
        mask_st = at("mask_st", M + 1.5, [P, P], F32R)
        mask_strict = at("mask_strict", M + 2, [P, P], F32R)
        one_st = at("one_st", M + 2.5, [P, P])
        one_strict = at("one_strict", M + 3, [P, P])
        neg_suffix = at("neg_suffix", M + 3.5, [P, P])
        neg_ones = at("neg_ones", M + 4, [P, P])
        gain_row = at("gain_row", M + 4.5, [P, D])
        mod_acc = at("mod_acc", M + 8.5, [P, 2, 512])
        mod_raw = at("mod_raw", M + 12.5, [P, 2, 512])
        row_a = at("row_a", M + 16.5, [HEADS, TOK])
        row_b = at("row_b", M + 18.5, [HEADS, TOK])
        silu_t = at("silu_t", M + 16.5, [P, 2, TOK])
        S0 = M + 20.5
        places = [S0]

        def small(name, n, dt=F32, parts=P):
            t = at(name, places[0], [parts, n], dt)
            places[0] += (n * 4 + 31) // 32 * 32 / KB
            return t

        wf = small("wf", 64)
        wf_hi = small("wf_hi", 64, F32R)
        wf_lo = small("wf_lo", 64, F32R)
        wf2 = small("wf2", 64)
        wf2_hi = small("wf2_hi", 64, F32R)
        wf2_lo = small("wf2_lo", 64, F32R)
        gain_1 = small("gain_1", KD)
        gain_2 = small("gain_2", KD)
        gain_3 = small("gain_3", KD)
        gain_4 = small("gain_4", KD)
        sgu_g = small("sgu_g", KD)
        bias_f = small("bias_f", 1)
        bias_dt = small("bias_dt", 1)
        a_log = small("a_log", 1)
        a_neg = small("a_neg", 1)
        c_col = small("c_col", KD)
        c_silu = small("c_silu", KD)
        shift_col = [small(f"shift{n}", KD) for n in (1, 2)]
        conv_w = small("conv_w", 6 * CONV_K)
        conv_b = small("conv_b", 6)
        short_w = small("short_w", 2 * SHORT_K)
        d_col = small("d_col", 4)
        norm_w = small("norm_w", 4)
        head_sel = small("head_sel", HEADS, F32R, 64)
        zeros_st = small("zeros_st", 1, F32R)
        power = small("power", 1)
        bn6 = small("bn6", NT * 2 * 6)
        mean_var = small("mean_var", NT * 2)
        mean_sq = small("mean_sq", NT)
        inv_rms = small("inv_rms", NT)
        neg_max = small("neg_max", 2)
        row_sum = small("row_sum", 2)
        row_inv = small("row_inv", 2)
        ms_ssm = small("ms_ssm", 2 * NT)
        rr_ssm = small("rr_ssm", 2 * NT)
        dt_col = small("dt_col", NT * HEADS)
        nacs_col = small("nacs_col", NT * HEADS)
        assert base + places[0] * KB <= 229344, places
        bank = ctx.enter_context(nc.psum_tensor("bank", [P, 8, 512], F32))

        def sems(*names):
            return [sem(n) for n in names]

        raw_in = sems("raw_in0", "raw_in1")
        hi_done, lo_done = sems("hi_done", "lo_done")
        acc_full, mid_used = sems("acc_full", "mid_used")
        emptied = sems(*(f"emptied{b}" for b in range(4)))
        dve_chain, act_chain, pool_chain = sems("dve_chain", "act_chain", "pool_chain")
        consts, small_in, x_loaded, x_again, wf_split = sems("consts", "small_in", "x_loaded", "x_again", "wf_split")
        ms_ready, rms_ready, xn_ready, tr_ready = sems("ms_ready", "rms_ready", "xn_ready", "tr_ready")
        tmp_ready, h_hi_done, h_lo_done = sems("tmp_ready", "h_hi_done", "h_lo_done")
        stats_done = sem("stats_done")
        gain_in, y_scaled, y_gained, x_added, stored = sems("gain_in", "y_scaled", "y_gained", "x_added", "stored")
        c_ready, mod_zero, mod_b_in, mod_summed = sems("c_ready", "mod_zero", "mod_b_in", "mod_summed")
        mod_w_in = sems("mod_w_in0", "mod_w_in1")
        mod_read, mod_out = sems("mod_read", "mod_out")
        row_mm, row_lin, row_ln, row_ready, rows_turned, cols_ready = sems(
            "row_mm", "row_lin", "row_ln", "row_ready", "rows_turned", "cols_ready")
        rows_split = sem("rows_split")
        score_ready, max_ready, prob_ready, prob_scaled = sems("score_ready", "max_ready", "prob_ready", "prob_scaled")
        pt_ready, pt_copied, pv_done, head_out, gated_b = sems("pt_ready", "pt_copied", "pv_done", "head_out", "gated_b")
        wsp_tr, wsp_done, v_normed, sgu_ready = sems("wsp_tr", "wsp_done", "v_normed", "sgu_ready")
        merged, merged_hi, merged_lo = sems("merged", "merged_hi", "merged_lo")
        act_hi_done, act_lo_done = sems("act_hi_done", "act_lo_done")
        pads_zero, conv_done, silu_x, z_silu = sems("pads_zero", "conv_done", "silu_x", "z_silu")
        z2_ready, ln_done, sp_ready, e_ready, att_ready, av_done, sb_hi_done, sb_lo_done = sems(
            "z2_ready", "ln_done", "sp_ready", "e_ready", "att_ready", "av_done", "sb_hi_done", "sb_lo_done")
        short_done, sc_hi_done, sc_lo_done = sems("short_done", "sc_hi_done", "sc_lo_done")
        xs_turned, xdt_done, cb_ready, cb_done = sems("xs_turned", "xdt_done", "cb_ready", "cb_done")
        dec_ready, dec_done, g_ready, ys_done, y_pair = sems("dec_ready", "dec_done", "g_ready", "ys_done", "y_pair")
        y_gated, sq_done, ss_ready, ms2_ready, rr_ready = sems("y_gated", "sq_done", "ss_ready", "ms2_ready", "rr_ready")
        rr_diags, rr_spread = sems("rr_diags", "rr_spread")
        y_normed, ssm_hi_done, ssm_lo_done = sems("y_normed", "ssm_hi_done", "ssm_lo_done")
        m2_ready, m2_hi_done, m2_lo_done = sems("m2_ready", "m2_hi_done", "m2_lo_done")

        def wait(eng, s, value):
            if not isinstance(value, int) or value > 0:
                eng.wait_ge(s, value)

        def wait_used(eng, n, pace=STILL):
            if n < 0:
                assert pace is STILL
                return
            kind, value = UNITS[n]["used"]
            if kind == "full":
                wait(eng, acc_full, value + pace.by(4 * pace.rounds))
            else:
                wait(eng, mid_used, value + pace.by(pace.mids))

        def wait_full(eng, n, b, pace=STILL):
            wait(eng, acc_full, UNITS[n]["full"] + b + 1 + pace.by(4 * pace.rounds))

        def wait_emptied(eng, n, b, pace=STILL):
            u = UNITS[n]
            wait(eng, emptied[2 * u["half"] + b], u["round"] + 1 + pace.by(pace.rounds))

        def ktiles(t, k, width):
            return t[:, :].rearrange("p (k c) -> p k c", c=width)[:, 0:k, :]

        class Chain:

            def __init__(self, eng, s):
                self.eng, self.sem, self.count, self.turn, self.each = eng, s, 0, None, 0

            def then(self, ins):
                self.count += 1
                ins.then_inc(self.sem, 1)
                self.wait()

            def wait(self):
                v = self.count if self.turn is None else self.count + self.turn * self.each
                self.eng.wait_ge(self.sem, v)

            def enter(self, turn, each):
                self.turn, self.each, self.first = turn, each, self.count

            def leave(self, turns):
                assert self.count - self.first == self.each
                self.count, self.turn = self.first + turns * self.each, None

        def two_chunks(eng, n0, units, pace_of, body):
            if n0 + 2 * units == len(UNITS):
                for c in range(2):
                    body(n0 + units * c, c, STILL)
            else:
                with eng.Fori(0, 2) as c:
                    body(n0, c, pace_of(c))

        n_q, n_k, n_va, n_g, n_vs, n_u = (FIRST[s] for s in ("q", "k", "va", "gates", "vs", "u"))
        n_out, n_up, n_dn = FIRST["out"], FIRST["up"], FIRST["down"]
        n_qk2, n_v2, n_x, n_z, n_sc = (FIRST[s] for s in ("sbqk", "sbv", "xbc", "z", "sc"))
        n_mg, n_out2, n_up2, n_dn2 = FIRST["merge"], FIRST["out2"], FIRST["up2"], FIRST["down2"]
        WIDTH = [TOK - P * j for j in range(NT)]
        START = [sum(WIDTH[:j]) for j in range(NT)]
        ATT_TASKS = [(h, i) for h in range(HEADS) for i in range(NT)]
        SB_TASKS = [(h, j) for h in range(SB_HEADS) for j in reversed(range(NT))]
        SSD_TASKS = [(h, j) for h in range(HEADS) for j in range(NT)]
        MOD_PAIRS = [(0, 1), (2, 3), (6, 7), (8, 9), (4, 5), (10, 11)]
        NORM_AT, POST_AT, LN_AT = [0, 12, 20, 28], [8, 16, 24, 32], 4

        SMALL = 25

        block = ctx.enter_context(nc.Block())

        @block.sync
        def _(sp):
            def kview(name):
                return a[name][0].rearrange("(k p) n -> p k n", p=P)

            w_in, w_in2 = kview("w_in"), kview("w_in_2")

            def free(n, pace=STILL):
                wait(sp, lo_done, n - 1 + pace.by(pace.units))

            def load(n, dst, src):
                sp.dma_start(dst, src).then_inc(raw_in[UNITS[n]["slot"]], 16)

            def load_f(n, w, col, pace=STILL):
                free(n, pace)
                r = ktiles(raw[UNITS[n]["slot"]], 8, 256)
                for k in (0, 4):
                    load(n, r[:, k:k + 4, :], w[:, k:k + 4, bass.ds(col, 256)])

            def load_t(n, w, k0, col, pace):
                free(n, pace)
                kt = UNITS[n]["kt"]
                r = ktiles(raw[UNITS[n]["slot"]], kt, 512)
                for k in (0, kt // 2):
                    load(n, r[:, k:k + kt // 2, :], w[:, k0 + k:k0 + k + kt // 2, bass.ds(col, 512)])

            def stream_f(n0, w, col0, turns):
                with sp.Fori(0, turns) as i:
                    for j in range(2):
                        load_f(n0 + j, w, 512 * i + (col0 + 256 * j), pair_pace(i))

            def stream_t(n0, w, col0):
                with sp.Fori(0, 2) as c:
                    for j in range(2):
                        load_t(n0 + j, w, 4 * j, 512 * c + col0, chunk_pace(c))

            def stream_up(n0, wg, wu, up_col):
                with sp.Fori(0, KF // 2) as i:
                    for j in range(2):
                        free(n0 + j, pair_pace(i))
                        r = ktiles(raw[UNITS[n0 + j]["slot"]], 8, 256)
                        load(n0 + j, r[:, :, 0:P], wg[:, :, bass.ds(256 * i + P * j, P)])
                        load(n0 + j, r[:, :, P:2 * P], wu[:, :, bass.ds(256 * i + (up_col + P * j), P)])

            def stream_down(n0, w):
                with sp.Fori(0, 2) as c:
                    for j in range(6):
                        load_t(n0 + j, w, 4 * j, 512 * c, down_pace(c))

            def next_gain(name, k):
                sp.wait_ge(y_gained, NT * k)
                sp.dma_start(gain_row[:], a[name][0].partition_broadcast(P)).then_inc(gain_in, 16)

            x_v = a["x"][0].rearrange("(t p) n -> p t n", p=P)
            sp.dma_start(x_in[:, 0:2, :], x_v[:, 0:2, :]).then_inc(x_loaded, 16)
            sp.dma_start(x_in[:, 2:4, :], x_v[:, 2:4, :]).then_inc(x_again, 16)
            for j in range(4):
                load_f(n_q + j, w_in, Q_COL + 256 * j)
            stream_f(n_k, w_in, K_COL, 2)
            stream_t(n_va, w_in, VA_COL)
            stream_f(n_g, w_in, GA_COL, 4)
            stream_t(n_vs, w_in, VS_COL)
            stream_f(n_u, w_in, U_COL, 2)
            stream_t(n_out, kview("w_out"), 0)
            sp.wait_ge(merged, KD)
            sp.dma_start(x_in[:], x_v).then_inc(x_again, 16)
            stream_up(n_up, kview("w_gate"), kview("w_up"), 0)
            next_gain("ffn_post_g", 1)
            stream_down(n_dn, kview("w_down"))
            for j in range(2):
                load_f(n_qk2 + j, w_in2, SBQ_COL + 256 * j)
            next_gain("g_post_mix_2", 2)
            load_f(n_v2, w_in2, SBV_COL)
            for j in range(3):
                load_f(n_x + j, w_in2, XBC_COL + 256 * j)
            for j in range(2):
                load_f(n_z + j, w_in2, Z_COL + 256 * j)
            for j in range(3):
                load_f(n_sc + j, w_in2, SC_COL + 256 * j)
            w_sc2, w_sb2, w_ssm2 = kview("w_sc_out_2"), kview("w_sb_out_2"), kview("w_ssm_out_2")
            for p in range(4):
                n = n_mg + 4 * p + 3
                for g in range(3):
                    load_f(n - 3 + g, w_in2, 256 * p + (GATE_COL + D * g))
                free(n)
                r = ktiles(raw[UNITS[n]["slot"]], 8, 256)
                load(n, r[:, 0:2, :], w_sc2[:, :, bass.ds(256 * p, 256)])
                load(n, r[:, 2:4, :], w_sb2[:, :, bass.ds(256 * p, 256)])
                load(n, r[:, 4:8, :], w_ssm2[:, :, bass.ds(256 * p, 256)])
            stream_t(n_out2, kview("w_o_2"), 0)
            w_ff2 = kview("w_ffn_in_2")
            stream_up(n_up2, w_ff2, w_ff2, FF)
            next_gain("g_post_ffn_2", 3)
            stream_down(n_dn2, kview("w_ffn_out_2"))
            out_v = out[0].rearrange("(t p) n -> t p n", p=P)
            for t in range(NT):
                sp.wait_ge(x_added, NT * 3 + t + 1)
                sp.dma_start(out_v[t], x_res[:, t, :]).then_inc(stored, 16)
            sp.wait_ge(stored, 16 * NT)

        @block.gpsimd
        def _(gp):
            chain = Chain(gp, pool_chain)
            then = chain.then

            for t, keep, fill, step, mult, op in (
                    (ident_r, 1.0, 0.0, -1, 1, ALU.is_equal),
                    (mask_qk, 0.0, MASKED, -1, 1, ALU.is_ge),
                    (mask_st, 0.0, MASKED, 1, -1, ALU.is_ge),
                    (mask_strict, 0.0, MASKED, 1, -1, ALU.is_gt),
                    (one_st, 1.0, 0.0, 1, -1, ALU.is_ge),
                    (one_strict, 1.0, 0.0, 1, -1, ALU.is_gt),
                    (neg_suffix, -1.0, 0.0, -1, 1, ALU.is_ge)):
                then(gp.memset(mod_acc[:, 0, 0:P], keep))
                then(gp.affine_select(out=t[:], in_=mod_acc[:, 0, 0:P], compare_op=op, fill=fill, base=0,
                                      pattern=[[step, P]], channel_multiplier=mult))
            then(gp.tensor_tensor(head_sel[:], ident[0:64, 0:HEADS], ident[0:64, 32:32 + HEADS], ALU.add))
            then(gp.memset(ones[:], 1.0))
            then(gp.memset(neg_ones[:], -1.0))
            then(gp.tensor_scalar(zeros_st[:], ones[:, 0:1], 0.0, None, ALU.mult))
            gp.memset(power[:], -0.5).then_inc(consts, 1)
            gp.wait_ge(consts, 1)

            def roots(first):
                for t in range(NT):
                    gp.wait_ge(ms_ready, first + t + 1)
                    then(gp.tensor_scalar(mean_sq[:, t:t + 1], mean_sq[:, t:t + 1], EPS, None, ALU.add))
                    gp.tensor_tensor(inv_rms[:, t:t + 1], mean_sq[:, t:t + 1], power[:], ALU.pow).then_inc(rms_ready, 1)

            def residual(k, y, old):
                roots(POST_AT[k])
                if k == 0:
                    gp.wait_ge(x_again, 32)
                for t in range(NT):
                    gp.wait_ge(y_gained, NT * k + t + 1)
                    gp.tensor_tensor(x_res[:, t, :], y[:, t, :], old[:, t, :], ALU.add).then_inc(x_added, 1)
                if k < 3:
                    roots(NORM_AT[k + 1])

            mod_w = a["mod_w_2"][0].rearrange("(k p) n -> k p n", p=P)

            def mod_pair(pair):
                for which, chunk in enumerate(MOD_PAIRS[pair]):
                    m, col = 2 * pair + which, 512 * chunk
                    acc = mod_acc[:, which, :]
                    wait(gp, mod_read, pair)
                    gp.memset(acc, 0.0).then_inc(mod_zero, 1)
                    gp.wait_ge(mod_zero, m + 1)
                    gp.dma_start(mod_acc[0:1, which, :], a["mod_b_2"][:, col:col + 512]).then_inc(mod_b_in, 16)
                    for k in range(KD):
                        s, step = k % 2, KD * m + k
                        for ahead in ([0, 1] if k == 0 else [k + 1] if k + 1 < KD else []):
                            gp.dma_start(mod_raw[:, ahead % 2, :], mod_w[ahead, :, col:col + 512]).then_inc(mod_w_in[ahead % 2], 16)
                        gp.wait_ge(mod_w_in[s], 16 * (step // 2 + 1))
                        then(gp.tensor_scalar(mod_raw[:, s, :], mod_raw[:, s, :], c_silu[:, k:k + 1], None, ALU.mult))
                        if k == 0:
                            gp.wait_ge(mod_b_in, 16 * (m + 1))
                        ins = gp.tensor_tensor(acc, acc, mod_raw[:, s, :], ALU.add)
                        if k + 1 < KD:
                            then(ins)
                        else:
                            ins.then_inc(mod_summed, 1)
                            gp.wait_ge(mod_summed, m + 1)

            roots(NORM_AT[0])
            gp.wait_ge(c_ready, 1)
            mod_pair(0)
            for f in range(KD):
                wait_emptied(gp, n_g + 4 + f // 2, f % 2)
                then(gp.tensor_scalar(gates[:, KD + f, :], gates[:, KD + f, :], 1.0, None, ALU.add))
            for f in range(KD):
                gp.wait_ge(head_out, f + 1)
                gp.tensor_tensor(q_t[:, f, :], q_t[:, f, :], gates[:, KD + f, :], ALU.mult).then_inc(gated_b, 1)
            roots(LN_AT)
            mod_pair(1)
            residual(0, y_out, x_in)
            mod_pair(2)
            mod_pair(3)
            residual(1, y_down, x_res)
            mod_pair(4)
            for c in range(4):
                gp.wait_ge(y_gated, c + 1)
                gp.tensor_tensor(z_t[:, c, :], y_ssm[:, c, :], y_ssm[:, c, :], ALU.mult).then_inc(sq_done, 1)
            gp.wait_ge(ms2_ready, 1)
            gp.tensor_tensor(rr_ssm[:], ms_ssm[:], power[:, 0:1].to_broadcast([P, 2 * NT]), ALU.pow).then_inc(rr_ready, 1)
            residual(2, y_out, x_res)
            mod_pair(5)
            residual(3, y_down, x_res)

        @block.scalar
        def _(act):
            then = Chain(act, act_chain).then

            def col(name):
                return a[name][0].rearrange("(k p) -> p k", p=P)

            with nc.allow_non_contiguous_dma(reason="a few hundred scalars, once"):
                loads = [
                    (c_col[:], col("c_2")), (gain_1[:], col("mix_pre_g")),
                    (wf[:, :].rearrange("p (k n) -> p k n", n=8), a["w_in"][0].rearrange("(k p) n -> p k n", p=P)[:, :, F_COL:F_COL + 8]),
                    (wf2[:, :].rearrange("p (k n) -> p k n", n=8), a["w_in_2"][0].rearrange("(k p) n -> p k n", p=P)[:, :, DT_COL:DT_COL + 8]),
                    (gain_2[:], col("ffn_pre_g")), (gain_3[:], col("g_pre_mix_2")), (gain_4[:], col("g_pre_ffn_2")),
                    (sgu_g[:], col("sgu_norm_g")),
                    (bias_f[0:HEADS, :], a["b_forget"].rearrange("a h -> h a")),
                    (a_log[0:HEADS, :], a["ssm_a_log_2"].rearrange("a h -> h a")),
                    (bias_dt[0:HEADS, :], a["ssm_dt_bias_2"].rearrange("a h -> h a")),
                    (conv_b[:], col("ssm_conv_b_2")), (norm_w[:], col("ssm_norm_w_2")),
                    (w_sp[:], a["w_spatial"][0].rearrange("g t s -> t g s")),
                    (gain_row[:], a["mix_post_g"][0].partition_broadcast(P)),
                    (b_sp[:], a["b_spatial"][0].partition_broadcast(P)),
                ]
                for k in range(CONV_K):
                    loads.append((conv_w[:, 6 * k:6 * k + 6], a["ssm_conv_w_2"][0, k].rearrange("(c p) -> p c", p=P)))
                for k in range(SHORT_K):
                    loads.append((short_w[:, 2 * k:2 * k + 2], a["sc_conv_w_2"][0, k].rearrange("(c p) -> p c", p=P)))
                for half in range(2):
                    loads.append((d_col[64 * half:64 * half + 64, :],
                                  a["ssm_d_2"][0].rearrange("(t h) -> h t", h=2)[half].partition_broadcast(64)))
                assert len(loads) == SMALL
                for dst, src in loads:
                    act.dma_start(dst, src).then_inc(small_in, 16)

            def split(n, pace=STILL):
                if n >= len(UNITS):
                    return
                u = UNITS[n]
                s, size = u["slot"], 512 * u["kt"]
                wait(act, raw_in[s], u["raw"] + pace.by(pace.raw[s]))
                wait_used(act, n - 2, pace)
                act.copy(w_hi[s][:, 0:size], raw[s][:, 0:size]).then_inc(hi_done, 1)

            def norm(c, x, xn):
                for t in range(NT):
                    act.wait_ge(rms_ready, NORM_AT[c] + t + 1)
                    act.activation(xn[:, t, :], x[:, t, :], ACT.Copy, scale=inv_rms[:, t:t + 1]).then_inc(xn_ready, 1)
                for k in range(KD):
                    act.wait_ge(tmp_ready, KD * c + k + 1)
                    act.copy(h_hi[:, k, :], h_tmp[:, k % 2, :]).then_inc(h_hi_done, 1)

            def post(k, y):
                for t in range(NT):
                    act.wait_ge(rms_ready, POST_AT[k] + t + 1)
                    act.activation(y[:, t, :], y[:, t, :], ACT.Copy, scale=inv_rms[:, t:t + 1]).then_inc(y_scaled, 1)

            def take(n, b, dst, pace=STILL, func=ACT.Copy, scale=1.0):
                wait_full(act, n, b, pace)
                act.activation(dst, bank[:, 2 * UNITS[n]["half"] + b, :], func, scale=scale).then_inc(
                    emptied[2 * UNITS[n]["half"] + b], 1)

            def chunks(n0, y, units, pace_of, func=ACT.Copy):
                def chunk(n, c, pace):
                    for j in range(units):
                        split(n + j + 1, pace)
                    for t in range(NT):
                        take(n + units - 1, t, y[:, t, bass.ds(512 * c, 512)], pace, func)

                two_chunks(act, n0, units, pace_of, chunk)

            def hidden(n0, which):
                act.preload_act_table(ACT.Silu)
                with act.Fori(0, KF // 2) as i:
                    pace = pair_pace(i)
                    for j in range(2):
                        n = n0 + j
                        split(n + 1, pace)
                        take(n, 0, silu_t[:, j, :], pace, ACT.Silu)
                        wait_emptied(act, n, 1, pace)
                        act.copy(act_hi[:, bass.ds(2 * i + j, 1), :].rearrange("p a n -> p (a n)"),
                                 bank[:, 4 + j, :]).then_inc(act_hi_done, 1)

            def softplus_tail():
                rb = row_b[0:HEADS, :]
                then(act.activation(rb, row_a[0:HEADS, :], ACT.Abs))
                then(act.activation(rb, rb, ACT.Exp, scale=-1.0))
                act.activation(rb, rb, ACT.Ln, bias=1.0).then_inc(row_ln, 1)

            act.wait_ge(small_in, 16 * SMALL)
            act.activation(c_silu[:], c_col[:], ACT.Silu).then_inc(c_ready, 1)
            act.copy(wf_hi[:], wf[:]).then_inc(wf_split, 1)
            act.copy(wf2_hi[:], wf2[:]).then_inc(wf_split, 1)
            act.preload_act_table_set("natural_log_exp_and_others")
            then(act.activation(a_neg[0:HEADS, :], a_log[0:HEADS, :], ACT.Exp))
            split(0)
            norm(0, x_in, xn_1)
            for j in range(4):
                split(n_q + j + 1)
                take(n_q + j, 0, q_t[:, 2 * j, :], STILL, ACT.Copy, float(P) ** -0.5)
            with act.Fori(0, 2) as i:
                pace = pair_pace(i)
                for j in range(2):
                    split(n_k + j + 1, pace)
                    dst = k_t[:, bass.ds(4 * i + 2 * j, 1), :]
                    take(n_k + j, 0, dst.rearrange("p a n -> p (a n)"), pace)
            chunks(n_va, v_att, 2, chunk_pace)
            act.wait_ge(row_lin, 1)
            softplus_tail()
            for s, (h, i) in enumerate(ATT_TASKS):
                n, w = n_g + h, P * (i + 1)
                act.wait_ge(max_ready, s + 1)
                wait(act, pt_ready, s - 1)
                act.activation(prob[:, s % 2, 0:w], bank[:, 4 + s % 2, 0:w], ACT.Exp, bias=neg_max[:, s % 2:s % 2 + 1],
                               accum_out=row_sum[:, s % 2:s % 2 + 1]).then_inc(prob_ready, 1)
                if i == 0:
                    if h > 0:
                        take(n - 1, 1, gates[:, 2 * h - 1, :], STILL, ACT.Tanh, 0.5)
                    split(n + 1)
                if i == 2:
                    take(n, 0, gates[:, 2 * h, :], STILL, ACT.Tanh, 0.5)
            take(n_vs - 1, 1, gates[:, 2 * KD - 1, :], STILL, ACT.Tanh, 0.5)
            act.preload_act_table(ACT.Gelu_apprx_tanh)
            chunks(n_vs, v_sgu, 2, chunk_pace, ACT.Gelu_apprx_tanh)
            for f in range(KD):
                n = n_u + f // 2
                if f % 2 == 0:
                    split(n + 1)
                wait(act, merged, f - 1)
                if f == 0:
                    act.wait_ge(gated_b, KD)
                take(n, f % 2, u_act[:, f % 2, :], STILL, ACT.Gelu_apprx_tanh)
                act.wait_ge(merged, f + 1)
                act.activation(mrg_hi[:, f, :], m_tmp[:, f % 2, :], ACT.Copy, scale=0.5).then_inc(merged_hi, 1)
            chunks(n_out, y_out, 2, chunk_pace)
            post(0, y_out)
            norm(1, x_res, xn_2)
            hidden(n_up, 0)
            chunks(n_dn, y_down, 6, down_pace)
            post(1, y_down)
            norm(2, x_res, xn_1)
            for j in range(2):
                split(n_qk2 + j + 1)
                take(n_qk2 + j, 0, qk2[:, 2 * j, :], STILL, ACT.Copy, SSM_HD ** -0.5 if j == 0 else 1.0)
            split(n_v2 + 1)
            for t in range(0, NT, 2):
                wait_full(act, n_v2, t)
                act.copy(v2[:, t, :], bank[:, t, 0:256]).then_inc(emptied[t], 1)
            act.preload_act_table_set("natural_log_exp_and_others")
            act.wait_ge(row_lin, 2)
            softplus_tail()
            for j in range(3):
                split(n_x + j + 1)
                take(n_x + j, 0, xbc_raw[:, 2 * j, PAD:PAD + TOK])
            for s in range(len(SB_TASKS) + 1):
                if s < len(SB_TASKS):
                    h, j = SB_TASKS[s]
                    w, z, t = WIDTH[j], bank[:, 4 + s % 2, :], sp_tmp[:, s % 2, :]
                    act.wait_ge(z2_ready, s + 1)
                    wait(act, sp_ready, s - 1)
                    then(act.activation(t[:, 0:w], z[:, 0:w], ACT.Abs))
                    then(act.activation(t[:, 0:w], t[:, 0:w], ACT.Exp, scale=-1.0))
                    act.activation(t[:, 0:w], t[:, 0:w], ACT.Ln, bias=1.0).then_inc(ln_done, 1)
                if s > 0:
                    w = WIDTH[SB_TASKS[s - 1][1]]
                    act.wait_ge(e_ready, s)
                    wait(act, av_done, s - 2)
                    act.activation(att[:, (s - 1) % 2, 0:w], bank[:, 4 + (s - 1) % 2, 0:w], ACT.Exp).then_inc(att_ready, 1)
                if s in (0, 8):
                    split(n_z + s // 8 + 1)
            for hp in range(2):
                act.wait_ge(av_done, 8 * (hp + 1))
                act.copy(sb_hi[:, hp, :], bank[:, 6 + hp, :]).then_inc(sb_hi_done, 1)
            act.preload_act_table(ACT.Silu)
            split(n_sc + 1)
            for c in (4, 5, 0, 1, 2, 3):
                act.wait_ge(conv_done, 6)
                act.activation(xs_t[:, c, :], xs_t[:, c, :], ACT.Silu).then_inc(silu_x, 1)
            for c in range(4):
                wait_emptied(act, n_z + c // 2, c % 2)
                act.activation(z_t[:, c, :], z_t[:, c, :], ACT.Silu).then_inc(z_silu, 1)
            take(n_sc, 0, sc_raw[:, 0, PAD:PAD + TOK])
            act.preload_act_table(ACT.Exp)
            for s in range(8):
                g, j = divmod(s, NT)
                act.wait_ge(cb_ready, s + 1)
                act.copy(cb[:, g, START[j]:START[j] + WIDTH[j]], bank[:, 4 + s % 4, 0:WIDTH[j]]).then_inc(cb_done, 1)
            for s, (h, j) in enumerate(SSD_TASKS):
                w = WIDTH[j]
                act.wait_ge(dec_ready, s + 1)
                wait(act, g_ready, s - 1)
                act.activation(decay[:, s % 2, 0:w], bank[:, 4 + s % 2, 0:w], ACT.Exp,
                               bias=nacs_col[:, HEADS * j + h:HEADS * j + h + 1]).then_inc(dec_done, 1)
                if s == 0:
                    split(n_sc + 2)
                if s == 16:
                    take(n_sc + 1, 0, sc_raw[:, 2, PAD:PAD + TOK])
                    split(n_mg)
            take(n_sc + 2, 0, sc_raw[:, 4, PAD:PAD + TOK])
            act.preload_act_table(ACT.Sigmoid)

            def gate_pair(n, g, pace):
                for f in range(2):
                    take(n, f, sig[:, 2 * g + f, :], pace, ACT.Sigmoid)

            def merged_hi_parts(pair, p, pace):
                for f in range(2):
                    act.wait_ge(m2_ready, 2 * pair + f + 1 + pace.by(2))
                    act.copy(m2_hi[:, bass.ds(2 * p + (2 * pair + f), 1), :].rearrange("p a n -> p (a n)"),
                             m2_tmp[:, f, :]).then_inc(m2_hi_done, 1)

            split(n_mg + 1)
            gate_pair(n_mg, 0, STILL)
            for c in range(2):
                act.wait_ge(short_done, c + 1)
                act.copy(sc_hi[:, c, :], sc_raw[:, 4 + c, PAD:PAD + TOK]).then_inc(sc_hi_done, 1)
            split(n_mg + 2)
            gate_pair(n_mg + 1, 1, STILL)
            split(n_mg + 3)
            for c in range(4):
                act.wait_ge(y_normed, c + 1)
                act.copy(ssm_hi[:, c, :], y_ssm[:, c, :]).then_inc(ssm_hi_done, 1)
            gate_pair(n_mg + 2, 2, STILL)
            split(n_mg + 4)
            merged_hi_parts(0, 0, STILL)
            with act.Fori(0, 3) as p:
                pace = merge_pace(p)
                for g in range(3):
                    split(n_mg + 4 + g + 1, pace)
                    gate_pair(n_mg + 4 + g, g, pace)
                split(n_mg + 8, pace)
                merged_hi_parts(1, p, pace)
            chunks(n_out2, y_out, 2, chunk_pace)
            post(2, y_out)
            norm(3, x_res, xn_2)
            hidden(n_up2, 1)
            chunks(n_dn2, y_down, 6, down_pace)
            post(3, y_down)

        @block.vector
        def _(dve):
            chain = Chain(dve, dve_chain)
            then = chain.then

            def split(n, pace=STILL):
                if n >= len(UNITS):
                    return
                u = UNITS[n]
                s, size = u["slot"], 512 * u["kt"]
                wait(dve, hi_done, n + 1 + pace.by(pace.units))
                dve.tensor_tensor(w_lo[s][:, 0:size], raw[s][:, 0:size], w_hi[s][:, 0:size].bitcast(F32),
                                  ALU.subtract).then_inc(lo_done, 1)

            def take(n, b, dst, pace=STILL):
                wait_full(dve, n, b, pace)
                dve.tensor_copy(dst, bank[:, 2 * UNITS[n]["half"] + b, :]).then_inc(emptied[2 * UNITS[n]["half"] + b], 1)

            def moments(t, square):
                mv = mean_var[:, 2 * t:2 * t + 2]
                then(dve.bn_aggr(mv, bn6[:, 12 * t:12 * t + 12]))
                if square:
                    ins = dve.scalar_tensor_tensor(mean_sq[:, t:t + 1], mv[:, 0:1], mv[:, 0:1], mv[:, 1:2], ALU.mult, ALU.add)
                else:
                    ins = dve.tensor_copy(mean_sq[:, t:t + 1], mv[:, 1:2])
                ins.then_inc(ms_ready, 1)

            def row_stats(x, t):
                dve.bn_stats(bn6[:, 12 * t:12 * t + 6], x[:, t, 0:512])
                then(dve.bn_stats(bn6[:, 12 * t + 6:12 * t + 12], x[:, t, 512:1024]))
                moments(t, True)

            def norm(c, gain, shift):
                def lo(k):
                    dve.wait_ge(h_hi_done, KD * c + k + 1)
                    dve.tensor_tensor(h_lo[:, k, :], h_tmp[:, k % 2, :], h_hi[:, k, :].bitcast(F32),
                                      ALU.subtract).then_inc(h_lo_done, 1)

                if shift is not None:
                    dve.wait_ge(mod_out, 2 * c - 2)
                for k in range(KD):
                    dve.wait_ge(tr_ready, KD * c + k + 1)
                    if k >= 2:
                        dve.wait_ge(h_lo_done, KD * c + k - 1)
                    src, dst = bank[:, 4 + k % 4, :], h_tmp[:, k % 2, :]
                    if shift is None:
                        ins = dve.tensor_scalar(dst, src, gain[:, k:k + 1], None, ALU.mult)
                    else:
                        ins = dve.tensor_scalar(dst, src, gain[:, k:k + 1], shift[:, k:k + 1], ALU.mult, ALU.add)
                    ins.then_inc(tmp_ready, 1)
                    if k > 0:
                        lo(k - 1)
                lo(KD - 1)

            def post(k, y):
                for t in range(NT):
                    moments(t, True)
                wait(dve, gain_in, 16 * k)
                if k >= 2:
                    dve.wait_ge(mod_out, 3 + k)
                for t in range(NT + 1):
                    if t < NT:
                        dve.wait_ge(y_scaled, NT * k + t + 1)
                        dve.tensor_tensor(y[:, t, :], y[:, t, :], gain_row[:], ALU.mult).then_inc(y_gained, 1)
                    if t > 0 and k < 3:
                        dve.wait_ge(x_added, NT * k + t)
                        row_stats(x_res, t - 1)

            def chunks(n0, y, units, pace_of):
                def chunk(n, c, pace):
                    for j in range(units):
                        split(n + j + 1, pace)
                    for t in range(NT):
                        wait_emptied(dve, n + units - 1, t, pace)
                        if y is not None:
                            stats = bn6[:, bass.ds(6 * c + 12 * t, 6)]
                            then_stats = dve.bn_stats(stats, y[:, t, bass.ds(512 * c, 512)])
                            if t == NT - 1:
                                then_stats.then_inc(stats_done, 1)

                two_chunks(dve, n0, units, pace_of, chunk)
                chunk_stats[0] += 2 if y is not None else 0
                wait(dve, stats_done, chunk_stats[0])

            def hidden(n0, which):
                with dve.Fori(0, KF // 2) as i:
                    pace = pair_pace(i)
                    for j in range(2):
                        n = n0 + j
                        split(n + 1, pace)
                        wait_emptied(dve, n, 0, pace)
                        wait_full(dve, n, 1, pace)
                        wait(dve, lo_done, n + 2 + pace.by(pace.units))
                        up = 2 * UNITS[n]["half"] + 1
                        dve.tensor_tensor(bank[:, 4 + j, :], bank[:, up, :], silu_t[:, j, :], ALU.mult).then_inc(emptied[up], 1)
                        dve.wait_ge(act_hi_done, KF * which + j + 1 + pace.by(2))
                        m = bass.ds(2 * i + j, 1)
                        dve.tensor_tensor(act_lo[:, m, :].rearrange("p a n -> p (a n)"), bank[:, 4 + j, :],
                                          act_hi[:, m, :].bitcast(F32).rearrange("p a n -> p (a n)"),
                                          ALU.subtract).then_inc(act_lo_done, 1)

            def mod_columns(pair, dst, scale):
                dve.wait_ge(mod_read, pair + 1)
                if scale:
                    ins = dve.scalar_tensor_tensor(dst[:], bank[:, 7, 0:KD], 1.0, dst[:], ALU.add, ALU.mult)
                else:
                    ins = dve.tensor_copy(dst[:], bank[:, 7, 0:KD])
                ins.then_inc(mod_out, 1)

            def mod_gate(pair, k):
                dve.wait_ge(gain_in, 16 * k)
                dve.wait_ge(mod_read, pair + 1)
                dve.tensor_tensor(gain_row[:, 0:512], gain_row[:, 0:512], bank[:, 4, :], ALU.mult)
                dve.tensor_tensor(gain_row[:, 512:1024], gain_row[:, 512:1024], bank[:, 5, :], ALU.mult).then_inc(mod_out, 1)

            def split_rows(src, dst):
                then(dve.tensor_scalar(dst[:], h_hi[0:64, 0, :].bitcast(F32), 0.0, None, ALU.mult))
                then(dve.tensor_copy(dst[0:HEADS, :], src))
                dve.tensor_tensor(dst[32:32 + HEADS, :], src, dst[0:HEADS, :].bitcast(F32), ALU.subtract).then_inc(rows_split, 1)

            chunk_stats = [0]
            assert SMALL == 25
            dve.wait_ge(wf_split, 2)
            dve.tensor_tensor(wf_lo[:], wf[:], wf_hi[:].bitcast(F32), ALU.subtract)
            dve.tensor_tensor(wf2_lo[:], wf2[:], wf2_hi[:].bitcast(F32), ALU.subtract).then_inc(wf_split, 1)
            dve.wait_ge(small_in, 16 * SMALL)
            for t in range(NT):
                dve.wait_ge(x_loaded if t < 2 else x_again, 16)
                row_stats(x_in, t)
            split(0)
            norm(0, gain_1, None)
            for n0, dst in ((n_q, q_t), (n_k, k_t)):
                with dve.Fori(0, 2) as i:
                    pace = pair_pace(i)
                    for j in range(2):
                        split(n0 + j + 1, pace)
                        d = dst[:, bass.ds(4 * i + (2 * j + 1), 1), :].rearrange("p a n -> p (a n)")
                        if n0 == n_q:
                            wait_full(dve, n0 + j, 1, pace)
                            b = 2 * UNITS[n0 + j]["half"] + 1
                            dve.tensor_scalar(d, bank[:, b, :], float(P) ** -0.5, None, ALU.mult).then_inc(emptied[b], 1)
                        else:
                            take(n0 + j, 1, d, pace)
            chunks(n_va, None, 2, chunk_pace)
            ra, rb = row_a[0:HEADS, :], row_b[0:HEADS, :]
            dve.wait_ge(row_mm, 1)
            dve.tensor_scalar(ra, bank[0:HEADS, 4, :], bias_f[0:HEADS, :], None, ALU.add).then_inc(row_lin, 1)
            dve.wait_ge(row_ln, 1)
            then(dve.scalar_tensor_tensor(ra, ra, 0.0, rb, ALU.min, ALU.subtract))
            then(dve.tensor_tensor_scan(rb, ra, ra, 0.0, ALU.add, ALU.bypass))
            then(dve.tensor_scalar(ra, rb, -1.0, None, ALU.mult))
            split_rows(ra, c_rows)
            for s in range(len(ATT_TASKS) + 3):
                if s >= 3 and ATT_TASKS[s - 3][1] == NT - 1:
                    dve.wait_ge(pv_done, s - 2)
                    dve.tensor_copy(q_t[:, ATT_TASKS[s - 3][0], :], bank[:, 7, :]).then_inc(head_out, 1)
                if s < len(ATT_TASKS):
                    h, i = ATT_TASKS[s]
                    w, b = P * (i + 1), s % 2
                    dve.wait_ge(score_ready, s + 1)
                    dve.tensor_reduce(neg_max[:, b:b + 1], bank[:, 4 + b, 0:w], AX_X, ALU.max, negate=True).then_inc(max_ready, 1)
                    dve.wait_ge(prob_ready, s + 1)
                    then(dve.reciprocal(row_inv[:, b:b + 1], row_sum[:, b:b + 1]))
                    dve.tensor_scalar(prob[:, b, 0:w], prob[:, b, 0:w], row_inv[:, b:b + 1], None, ALU.mult).then_inc(prob_scaled, 1)
                if 1 <= s <= len(ATT_TASKS):
                    w, b = P * (ATT_TASKS[s - 1][1] + 1), (s - 1) % 2
                    dve.wait_ge(pt_ready, s)
                    wait(dve, pv_done, s - 2)
                    dve.tensor_copy(prob_t[:, b, 0:w], bank[:, 6, 0:w]).then_inc(pt_copied, 1)
                if s < len(ATT_TASKS) and i == 0:
                    split(n_g + h + 1)
            mod_columns(0, shift_col[0], False)
            for g in range(0, HEADS, 4):
                dve.wait_ge(wsp_tr, g // 4 + 1)
                dve.tensor_tensor(w_sp_t[:, g:g + 4, :], bank[:, 4 + g // 4, :].rearrange("p (g t) -> p g t", t=P),
                                  one_st[:].unsqueeze(1).broadcast_to([P, 4, P]), ALU.mult).then_inc(wsp_done, 1)
            chunks(n_vs, v_sgu, 2, chunk_pace)
            split(n_u + 1)
            for t in range(NT):
                moments(t, False)
            for t in range(NT):
                dve.wait_ge(rms_ready, LN_AT + t + 1)
                dve.tensor_scalar(v_sgu[:, t, :], v_sgu[:, t, :], mean_var[:, 2 * t:2 * t + 1], inv_rms[:, t:t + 1],
                                  ALU.subtract, ALU.mult).then_inc(v_normed, 1)
            dve.wait_ge(gated_b, KD)
            for f in range(KD):
                n, m = n_u + f // 2, m_tmp[:, f % 2, :]
                if f % 2 == 0 and f > 0:
                    split(n + 1)
                dve.wait_ge(sgu_ready, f + 1)
                wait(dve, merged_hi, f - 1)
                then(dve.scalar_tensor_tensor(
                    m.rearrange("p (c t) -> p c t", t=P), bank[:, 4 + f % 2, :].rearrange("p (c t) -> p c t", t=P),
                    sgu_g[:, f:f + 1], b_sp[:, f, :].unsqueeze(1).broadcast_to([P, NT, P]), ALU.mult, ALU.add))
                wait_emptied(dve, n, f % 2)
                then(dve.tensor_tensor(m, m, u_act[:, f % 2, :], ALU.mult))
                then(dve.scalar_tensor_tensor(m, gates[:, f, :], 1.0, m, ALU.add, ALU.mult))
                dve.tensor_tensor(m, m, q_t[:, f, :], ALU.add).then_inc(merged, 1)
                dve.wait_ge(merged_hi, f + 1)
                dve.scalar_tensor_tensor(mrg_lo[:, f, :], m, 0.5, mrg_hi[:, f, :].bitcast(F32), ALU.mult,
                                         ALU.subtract).then_inc(merged_lo, 1)
            mod_columns(1, gain_3, True)
            chunks(n_out, y_out, 2, chunk_pace)
            post(0, y_out)
            norm(1, gain_2, None)
            hidden(n_up, 0)
            mod_columns(2, shift_col[1], False)
            chunks(n_dn, y_down, 6, down_pace)
            post(1, y_down)
            norm(2, gain_3, shift_col[0])
            for j in range(2):
                split(n_qk2 + j + 1)
                if j == 0:
                    wait_full(dve, n_qk2, 1)
                    b = 2 * UNITS[n_qk2]["half"] + 1
                    dve.tensor_scalar(qk2[:, 1, :], bank[:, b, :], SSM_HD ** -0.5, None, ALU.mult).then_inc(emptied[b], 1)
                else:
                    take(n_qk2 + j, 1, qk2[:, 3, :])
            split(n_v2 + 1)
            for t in range(1, NT, 2):
                wait_full(dve, n_v2, t)
                dve.tensor_copy(v2[:, t, :], bank[:, t, 0:256]).then_inc(emptied[t], 1)
            dve.memset(xbc_raw[:, :, 0:PAD], 0.0).then_inc(pads_zero, 1)
            dve.wait_ge(row_mm, 2)
            dve.tensor_scalar(ra, bank[0:HEADS, 4, :], bias_dt[0:HEADS, :], None, ALU.add).then_inc(row_lin, 1)
            dve.wait_ge(row_ln, 2)
            then(dve.scalar_tensor_tensor(ra, ra, 0.0, rb, ALU.max, ALU.add))
            then(dve.tensor_scalar(rb, ra, a_neg[0:HEADS, :], -1.0, ALU.mult, ALU.mult))
            dve.tensor_tensor_scan(rb, rb, rb, 0.0, ALU.add, ALU.bypass).then_inc(row_ready, 1)
            for j in range(3):
                split(n_x + j + 1)
                take(n_x + j, 1, xbc_raw[:, 2 * j + 1, PAD:PAD + TOK])
            dve.wait_ge(rows_turned, 1)
            dve.tensor_copy(dt_col[:], bank[:, 5, 0:NT * HEADS])
            dve.tensor_scalar(nacs_col[:], bank[:, 5, NT * HEADS:2 * NT * HEADS], -1.0, None, ALU.mult).then_inc(cols_ready, 1)
            mod_columns(3, gain_4, True)
            dve.wait_ge(pads_zero, 1)

            def convolve(c):
                wait_emptied(dve, n_x + c // 2, c % 2)
                for k in reversed(range(CONV_K)):
                    o = PAD - (CONV_K - 1) + k
                    x, w = xbc_raw[:, c, o:o + TOK], conv_w[:, 6 * k + c:6 * k + c + 1]
                    if k == CONV_K - 1:
                        then(dve.tensor_scalar(xs_t[:, c, :], x, w, conv_b[:, c:c + 1], ALU.mult, ALU.add))
                    elif k > 0:
                        then(dve.scalar_tensor_tensor(xs_t[:, c, :], x, w, xs_t[:, c, :], ALU.mult, ALU.add))
                    else:
                        dve.scalar_tensor_tensor(xs_t[:, c, :], x, w, xs_t[:, c, :], ALU.mult, ALU.add).then_inc(conv_done, 1)

            for s, (h, j) in enumerate(SB_TASKS):
                w, lo, z = WIDTH[j], START[j], bank[:, 4 + s % 2, :]
                dve.wait_ge(ln_done, s + 1)
                wait(dve, e_ready, NT * h)
                sp_j = sp_all[:, lo:lo + w]
                then(dve.scalar_tensor_tensor(sp_j, z[:, 0:w], 0.0, sp_tmp[:, s % 2, 0:w], ALU.max, ALU.add))
                dve.tensor_tensor(sp_j[:, 0:P], sp_j[:, 0:P], one_strict[:], ALU.mult).then_inc(sp_ready, 1)
                if s % 2 == 1 and s // 2 < 6:
                    convolve(s // 2)
                if s in (0, 8):
                    split(n_z + s // 8 + 1)
                if s in (3, 7, 11, 15):
                    f = s // 4
                    take(n_z + f // 2, f % 2, z_t[:, f, :])
            for hp in range(2):
                dve.wait_ge(sb_hi_done, hp + 1)
                dve.tensor_tensor(sb_lo[:, hp, :], bank[:, 6 + hp, :], sb_hi[:, hp, :].bitcast(F32), ALU.subtract).then_inc(sb_lo_done, 1)
            split(n_sc + 1)
            dve.wait_ge(av_done, len(SB_TASKS))
            dve.memset(sc_raw[:, 2:4, 0:PAD], 0.0).then_inc(pads_zero, 1)
            for j in range(NT):
                dve.wait_ge(xs_turned, j + 1)
                dve.tensor_tensor(xdt[:, j, :].rearrange("p (h d) -> p h d", d=SSM_HD),
                                  bank[:, 4 + j, :].rearrange("p (h d) -> p h d", d=SSM_HD),
                                  dt_col[:, HEADS * j:HEADS * j + HEADS].unsqueeze(2).broadcast_to([P, HEADS, SSM_HD]),
                                  ALU.mult).then_inc(xdt_done, 1)
            take(n_sc, 1, sc_raw[:, 1, PAD:PAD + TOK])
            dve.wait_ge(row_ready, 1)
            split_rows(rb, a_rows)

            def gate_z(c):
                dve.wait_ge(z_silu, c + 1)
                dve.wait_ge(y_pair, c + 1)
                dve.tensor_tensor(y_ssm[:, c, :], y_ssm[:, c, :], z_t[:, c, :], ALU.mult).then_inc(y_gated, 1)

            for s, (h, j) in enumerate(SSD_TASKS):
                w, g = WIDTH[j], h // 4
                dve.wait_ge(dec_done, s + 1)
                if s == 0:
                    dve.wait_ge(cb_done, 8)
                wait(dve, ys_done, s - 1)
                dve.tensor_tensor(g_ssd[:, s % 2, 0:w], decay[:, s % 2, 0:w], cb[:, g, START[j]:START[j] + w],
                                  ALU.mult).then_inc(g_ready, 1)
                if s == 0:
                    split(n_sc + 2)
                if s == 16:
                    take(n_sc + 1, 1, sc_raw[:, 3, PAD:PAD + TOK])
                    split(n_mg)
                if s % 8 == 2 and s > 8:
                    finish_pair = (s - 8) // 8
                    dve.wait_ge(ys_done, 8 * (finish_pair + 1))
                    dve.scalar_tensor_tensor(y_ssm[:, finish_pair, :], xs_t[:, finish_pair, :], d_col[:, finish_pair:finish_pair + 1],
                                             bank[:, 6 + finish_pair % 2, :], ALU.mult, ALU.add).then_inc(y_pair, 1)
                    gate_z(finish_pair)
            dve.wait_ge(ys_done, len(SSD_TASKS))
            dve.scalar_tensor_tensor(y_ssm[:, 3, :], xs_t[:, 3, :], d_col[:, 3:4], bank[:, 7, :], ALU.mult, ALU.add).then_inc(y_pair, 1)
            gate_z(3)
            take(n_sc + 2, 1, sc_raw[:, 5, PAD:PAD + TOK])
            split(n_mg + 1)
            wait_emptied(dve, n_sc + 1, 0)
            wait_emptied(dve, n_sc + 1, 1)
            wait_emptied(dve, n_sc + 2, 0)
            wait_emptied(dve, n_sc + 2, 1)
            wait_emptied(dve, n_sc, 0)
            wait_emptied(dve, n_sc, 1)
            for c in range(2):
                p_, o_ = sc_raw[:, 2 + c, :], sc_raw[:, 4 + c, PAD:PAD + TOK]
                then(dve.tensor_tensor(p_[:, PAD:PAD + TOK], p_[:, PAD:PAD + TOK], o_, ALU.mult))
                then(dve.tensor_scalar(o_, p_[:, PAD:PAD + TOK], short_w[:, 4 + c:5 + c], None, ALU.mult))
                then(dve.scalar_tensor_tensor(o_, p_[:, PAD - 1:PAD - 1 + TOK], short_w[:, 2 + c:3 + c], o_, ALU.mult, ALU.add))
                then(dve.scalar_tensor_tensor(o_, p_[:, PAD - 2:PAD - 2 + TOK], short_w[:, c:c + 1], o_, ALU.mult, ALU.add))
                dve.tensor_tensor(o_, o_, sc_raw[:, c, PAD:PAD + TOK], ALU.mult).then_inc(short_done, 1)
            for c in range(2):
                dve.wait_ge(sc_hi_done, c + 1)
                dve.tensor_tensor(sc_lo[:, c, :], sc_raw[:, 4 + c, PAD:PAD + TOK], sc_hi[:, c, :].bitcast(F32), ALU.subtract).then_inc(sc_lo_done, 1)
            dve.wait_ge(ss_ready, 1)
            dve.tensor_scalar(ms_ssm[:], bank[:, 4, 0:2 * NT], 1.0 / 256, EPS, ALU.mult, ALU.add).then_inc(ms2_ready, 1)
            split(n_mg + 2)
            dve.wait_ge(rr_ready, 1)
            for q in range(2 * NT):
                ins = dve.tensor_scalar(rr_diag[:, q, :], ident[:], rr_ssm[:, q:q + 1], None, ALU.mult)
            ins.then_inc(rr_diags, 1)
            split(n_mg + 3)
            for c in range(4):
                dve.wait_ge(rr_spread, c // 2 + 1)
                dve.scalar_tensor_tensor(y_ssm[:, c, :], y_ssm[:, c, :], norm_w[:, c:c + 1], bank[:, 4 + c // 2, :],
                                         ALU.mult, ALU.mult).then_inc(y_normed, 1)
            for c in range(4):
                dve.wait_ge(ssm_hi_done, c + 1)
                dve.tensor_tensor(ssm_lo[:, c, :], y_ssm[:, c, :], ssm_hi[:, c, :].bitcast(F32), ALU.subtract).then_inc(ssm_lo_done, 1)
            def merge(n, pair, p, pace):
                for g in range(3):
                    for f in range(2):
                        wait_emptied(dve, n + g, f, pace)
                for f in range(2):
                    m = m2_tmp[:, f, :]
                    ga, gb, gc = (sig[:, 2 * g + f, :] for g in range(3))
                    wait_full(dve, n + 3, f, pace)
                    then(dve.tensor_tensor(m, gb, bank[:, 4 + 2 * f, :], ALU.mult))
                    then(dve.tensor_tensor(gc, gc, bank[:, 5 + 2 * f, :], ALU.mult))
                    then(dve.tensor_tensor(m, m, gc, ALU.add))
                    dve.tensor_tensor(ga, ga, bank[:, 2 + f, :], ALU.mult).then_inc(emptied[2 + f], 1)
                    wait_emptied(dve, n + 3, f, pace)
                    dve.tensor_tensor(m, m, ga, ALU.add).then_inc(m2_ready, 1)
                for f in range(2):
                    dve.wait_ge(m2_hi_done, 2 * pair + f + 1 + pace.by(2))
                    t = bass.ds(2 * p + (2 * pair + f), 1)
                    dve.tensor_tensor(m2_lo[:, t, :].rearrange("p a n -> p (a n)"), m2_tmp[:, f, :],
                                      m2_hi[:, t, :].bitcast(F32).rearrange("p a n -> p (a n)"), ALU.subtract).then_inc(m2_lo_done, 1)

            split(n_mg + 4)
            merge(n_mg, 0, 0, STILL)
            with dve.Fori(0, 3) as p:
                pace = merge_pace(p)
                chain.enter(p, 6)
                for g in range(4):
                    split(n_mg + 4 + g + 1, pace)
                merge(n_mg + 4, 1, p, pace)
            chain.leave(3)
            mod_gate(4, 2)
            chunks(n_out2, y_out, 2, chunk_pace)
            post(2, y_out)
            norm(3, gain_4, shift_col[1])
            hidden(n_up2, 1)
            mod_gate(5, 3)
            chunks(n_dn2, y_down, 6, down_pace)
            post(3, y_down)

        @block.tensor
        def _(pe):
            def three_passes(o, st_hi, st_lo, mv_hi, mv_lo, first, last):
                pe.matmul(o, st_hi, mv_hi, start=first, stop=False)
                pe.matmul(o, st_hi, mv_lo, start=False, stop=False)
                return pe.matmul(o, st_lo, mv_hi, start=False, stop=last)

            def feature_tile(n, f, pace=STILL, ks=range(KD), c=None):
                u = UNITS[n]
                b = 2 * u["half"] + f
                hi, lo = ktiles(w_hi[u["slot"]], 8, 256), ktiles(w_lo[u["slot"]], 8, 256)
                fs = slice(P * f, P * f + P)
                if ks[0] == 0:
                    wait(pe, lo_done, n + 1 + pace.by(pace.units))
                    wait(pe, emptied[b], u["round"] + pace.by(pace.rounds))
                for k in ks:
                    if c is not None:
                        pe.wait_ge(h_lo_done, KD * c + k + 1)
                    ins = three_passes(bank[:, b, :], hi[:, k, fs], lo[:, k, fs], h_hi[:, k, :], h_lo[:, k, :],
                                       k == 0, k == KD - 1)
                if ks[-1] == KD - 1:
                    ins.then_inc(acc_full, 1)

            def quarter(n, q):
                feature_tile(n, q // 2, ks=range(4 * (q % 2), 4 * (q % 2) + 4))

            def f_pairs(n0, turns, c=None):
                if c is not None:
                    for j in range(2):
                        for f in range(2):
                            feature_tile(n0 + j, f, c=c if (j, f) == (0, 0) else None)
                    n0, turns = n0 + 2, turns - 1
                with pe.Fori(0, turns) as i:
                    for j in range(2):
                        for f in range(2):
                            feature_tile(n0 + j, f, pair_pace(i))

            def token_unit(n, x_hi, x_lo, k0, first, last, pace, width=512):
                u = UNITS[n]
                kt = 8 if width == 256 else u["kt"]
                hi, lo = ktiles(w_hi[u["slot"]], kt, width), ktiles(w_lo[u["slot"]], kt, width)
                wait(pe, lo_done, n + 1 + pace.by(pace.units))
                for t in range(NT):
                    ts = slice(P * t, P * t + P)
                    if first:
                        wait(pe, emptied[t], u["round"] + pace.by(pace.rounds))
                    for k in range(kt):
                        ins = three_passes(bank[:, t, 0:width], x_hi[:, k0 + k, ts], x_lo[:, k0 + k, ts],
                                           hi[:, k, :], lo[:, k, :], first and k == 0, last and k == kt - 1)
                    if last:
                        ins.then_inc(acc_full, 1)
                if not last:
                    ins.then_inc(mid_used, 1)

            def chunks(n0, x_hi, x_lo, there=None, count=0):
                with pe.Fori(0, 2) as c:
                    for j in range(2):
                        if there is not None:
                            pe.wait_ge(there, count)
                        token_unit(n0 + j, x_hi, x_lo, 4 * j, j == 0, j == 1, chunk_pace(c))

            def down(n0, which):
                with pe.Fori(0, 2) as c:
                    for j in range(6):
                        pe.wait_ge(act_lo_done, KF * which + min(4 * j + 4, KF))
                        token_unit(n0 + j, act_hi, act_lo, 4 * j, j == 0, j == 5, down_pace(c))

            def turn(c, xn):
                pe.wait_ge(xn_ready, NT * c + NT)
                for k in range(KD):
                    if k >= 4:
                        pe.wait_ge(tmp_ready, KD * c + k - 3)
                    for t in range(NT):
                        ins = pe.transpose(bank[:, 4 + k % 4, P * t:P * t + P], xn[:, t, P * k:P * k + P], ident[:])
                    ins.then_inc(tr_ready, 1)

            def narrow(hi, lo):
                for k in range(KD):
                    ks = slice(8 * k, 8 * k + 8)
                    ins = three_passes(bank[0:HEADS, 4, :], hi[:, ks], lo[:, ks], h_hi[:, k, :], h_lo[:, k, :],
                                       k == 0, k == KD - 1)
                ins.then_inc(row_mm, 1)

            def mod_columns(pair):
                pe.wait_ge(mod_summed, 2 * pair + 2)
                for q in range(KD):
                    ins = pe.matmul(bank[:, 7, q:q + 1], mod_acc[:, q // 4, P * (q % 4):P * (q % 4) + P], ones[:, 0:1],
                                    start=True, stop=True)
                ins.then_inc(mod_read, 1)

            def mod_gate(pair):
                pe.wait_ge(mod_summed, 2 * pair + 2)
                for w in range(2):
                    ins = pe.matmul(bank[:, 4 + w, :], ones[:], mod_acc[:, w, :], start=True, stop=True)
                ins.then_inc(mod_read, 1)

            def head_row(h):
                return head_sel[:, h:h + 1].to_broadcast([64, P])

            pe.wait_ge(consts, 1)
            turn(0, xn_1)
            f_pairs(n_q, 2, c=0)
            f_pairs(n_k, 2)
            chunks(n_va, h_hi, h_lo)
            pe.wait_ge(wf_split, 3)
            narrow(wf_hi, wf_lo)
            for f in range(2):
                for n in (n_q + 2, n_q + 3, n_k + 2, n_k + 3):
                    wait_emptied(pe, n, f)
            for t in range(NT):
                wait_emptied(pe, n_va + 3, t)
            pe.wait_ge(rows_split, 1)
            for s in range(len(ATT_TASKS) + 2):
                if s < len(ATT_TASKS):
                    h, i = ATT_TASKS[s]
                    w, b = P * (i + 1), 4 + s % 2
                    wait(pe, prob_ready, s - 1)
                    pe.matmul(bank[:, b, 0:w], head_row(h), c_rows[:, 0:w], start=True, stop=False)
                    pe.matmul(bank[:, b, P * i:w], ident_r[:], mask_qk[:], start=False, stop=False)
                    pe.matmul(bank[:, b, 0:w], q_t[:, h, P * i:P * i + P], k_t[:, h, 0:w],
                              start=False, stop=True).then_inc(score_ready, 1)
                    quarter(n_g + h, i)
                if 1 <= s <= len(ATT_TASKS):
                    i, b = ATT_TASKS[s - 1][1], (s - 1) % 2
                    pe.wait_ge(prob_scaled, s)
                    wait(pe, pt_copied, s - 1)
                    for j in range(i + 1):
                        ins = pe.transpose(bank[:, 6, P * j:P * j + P], prob[:, b, P * j:P * j + P], ident[:])
                    ins.then_inc(pt_ready, 1)
                if s >= 2:
                    (h, i), b = ATT_TASKS[s - 2], (s - 2) % 2
                    pe.wait_ge(pt_copied, s - 1)
                    if i == 0:
                        wait(pe, head_out, h)
                    for j in range(i + 1):
                        ins = pe.matmul(bank[:, 7, P * i:P * i + P], v_att[:, j, P * h:P * h + P],
                                        prob_t[:, b, P * j:P * j + P], start=(j == 0), stop=(j == i))
                    ins.then_inc(pv_done, 1)
            pe.wait_ge(head_out, HEADS)
            mod_columns(0)
            pe.wait_ge(small_in, 16 * SMALL)
            for g in range(HEADS):
                ins = pe.transpose(bank[:, 4 + g // 4, P * (g % 4):P * (g % 4) + P], w_sp[:, g, :], ident[:])
                if g % 4 == 3:
                    ins.then_inc(wsp_tr, 1)
            chunks(n_vs, h_hi, h_lo)
            for f in range(KD):
                feature_tile(n_u + f // 2, f % 2)
                if f % 2 == 1:
                    pe.wait_ge(v_normed, NT)
                    pe.wait_ge(wsp_done, 2)
                    for g in (f - 1, f):
                        wait(pe, merged, g - 1)
                        for c in range(NT):
                            ins = pe.matmul(bank[:, 4 + g % 2, P * c:P * c + P], v_sgu[:, c, P * g:P * g + P], w_sp_t[:, g, :],
                                            start=True, stop=True)
                        ins.then_inc(sgu_ready, 1)
            pe.wait_ge(mod_out, 1)
            mod_columns(1)
            pe.wait_ge(merged_lo, KD)
            chunks(n_out, mrg_hi, mrg_lo)
            turn(1, xn_2)
            f_pairs(n_up, KF // 2, c=1)
            pe.wait_ge(mod_out, 2)
            mod_columns(2)
            down(n_dn, 0)
            turn(2, xn_1)
            for j in range(2):
                for f in range(2):
                    feature_tile(n_qk2 + j, f, c=2 if (j, f) == (0, 0) else None)
            pe.wait_ge(tmp_ready, 3 * KD)
            narrow(wf2_hi, wf2_lo)
            token_unit(n_v2, h_hi, h_lo, 0, True, True, STILL, 256)
            for f in range(2):
                feature_tile(n_x, f)
            pe.wait_ge(row_ready, 1)
            for r, row in ((0, row_a), (1, row_b)):
                for j in range(NT):
                    o = HEADS * (NT * r + j)
                    ins = pe.transpose(bank[:, 5, o:o + HEADS], row[0:HEADS, P * j:P * j + P], ident[0:HEADS, 0:HEADS])
            ins.then_inc(rows_turned, 1)
            for j in (1, 2):
                for f in range(2):
                    feature_tile(n_x + j, f)
            pe.wait_ge(mod_out, 3)
            mod_columns(3)
            pe.wait_ge(cols_ready, 1)
            pe.wait_ge(mod_out, 4)
            for f in range(2):
                wait_emptied(pe, n_qk2, f)
                wait_emptied(pe, n_qk2 + 1, f)
            for t in range(NT):
                wait_emptied(pe, n_v2, t)
            for s in range(len(SB_TASKS) + 2):
                if s < len(SB_TASKS):
                    h, j = SB_TASKS[s]
                    rows, w = slice(SSM_HD * (h % 2), SSM_HD * (h % 2) + SSM_HD), WIDTH[j]
                    wait(pe, att_ready, s - 1)
                    pe.matmul(bank[:, 4 + s % 2, 0:w], qk2[rows, 2 + h // 2, P * j:P * j + P], qk2[rows, h // 2, P * j:TOK],
                              start=True, stop=True).then_inc(z2_ready, 1)
                    if s % 2 == 0:
                        quarter(n_z + s // 8, (s // 2) % 4)
                if 1 <= s <= len(SB_TASKS):
                    (h, j), o = SB_TASKS[s - 1], bank[:, 4 + (s - 1) % 2, :]
                    w = WIDTH[j]
                    pe.wait_ge(sp_ready, s)
                    pe.matmul(o[:, 0:P], ident_r[:], mask_strict[:], start=False, stop=False, skip_group_check=True)
                    for j2 in range(j + 1, NT):
                        pe.matmul(o[:, P * (j2 - j):w], neg_ones[:], sp_all[:, START[j2]:START[j2] + WIDTH[j2]],
                                  start=False, stop=False, skip_group_check=True)
                    pe.matmul(o[:, 0:w], neg_suffix[:], sp_all[:, START[j]:START[j] + w], start=False, stop=True,
                              skip_group_check=True).then_inc(e_ready, 1)
                if s >= 2:
                    h, j = SB_TASKS[s - 2]
                    pe.wait_ge(att_ready, s - 1)
                    rows = slice(SSM_HD * (h % 2), SSM_HD * (h % 2) + SSM_HD)
                    if j == NT - 1 and h % 2 == 0:
                        pe.matmul(bank[:, 6 + h // 2, :], zeros_st[:].to_broadcast([P, P]), h_hi[:, 0, :], start=True, stop=False)
                    pe.matmul(bank[rows, 6 + h // 2, P * j:TOK], v2[:, j, SSM_HD * h:SSM_HD * h + SSM_HD], att[:, s % 2, 0:WIDTH[j]],
                              start=False, stop=(j == 0)).then_inc(av_done, 1)
            for f in range(2):
                feature_tile(n_sc, f)
            pe.wait_ge(silu_x, 6)
            pe.wait_ge(sb_lo_done, 2)
            for j in range(NT):
                for c in range(4):
                    ins = pe.transpose(bank[:, 4 + j, P * c:P * c + P], xs_t[:, c, P * j:P * j + P], ident[:])
                ins.then_inc(xs_turned, 1)
            for s in range(8):
                g, j = divmod(s, NT)
                rows = slice(SSM_HD * g, SSM_HD * g + SSM_HD)
                if s < 4:
                    pe.wait_ge(xdt_done, s + 1)
                else:
                    pe.wait_ge(cb_done, s - 3)
                pe.matmul(bank[:, 4 + s % 4, 0:WIDTH[j]], xs_t[rows, 4, P * j:P * j + P], xs_t[rows, 5, P * j:TOK],
                          start=True, stop=True).then_inc(cb_ready, 1)
            pe.wait_ge(cb_done, 8)
            pe.wait_ge(rows_split, 2)
            for s in range(len(SSD_TASKS) + 2):
                if s < len(SSD_TASKS):
                    (h, j), b = SSD_TASKS[s], 4 + s % 2
                    w = WIDTH[j]
                    wait(pe, dec_done, s - 1)
                    if w > P:
                        pe.matmul(bank[:, b, P:w], head_row(h), a_rows[:, P * j + P:TOK], start=True, stop=True)
                    pe.matmul(bank[:, b, 0:P], head_row(h), a_rows[:, P * j:P * j + P], start=True, stop=False)
                    pe.matmul(bank[:, b, 0:P], ident_r[:], mask_st[:], start=False, stop=True).then_inc(dec_ready, 1)
                    if s % 4 == 0:
                        quarter(n_sc + 1 + s // 16, (s // 4) % 4)
                if s >= 2:
                    h, j = SSD_TASKS[s - 2]
                    rows = slice(SSM_HD * (h % 2), SSM_HD * (h % 2) + SSM_HD)
                    pe.wait_ge(g_ready, s - 1)
                    if h % 2 == 0 and j == 0:
                        wait(pe, y_pair, h // 2 - 1)
                    pe.matmul(bank[rows, 6 + (h // 2) % 2, P * j:TOK], xdt[:, j, SSM_HD * h:SSM_HD * h + SSM_HD], g_ssd[:, s % 2, 0:WIDTH[j]],
                              start=(j == 0), stop=(j == NT - 1)).then_inc(ys_done, 1)
            def gate_unit(n, pace):
                for f in range(2):
                    feature_tile(n, f, pace)

            def branches(n, pace):
                u = UNITS[n]
                hi, lo = ktiles(w_hi[u["slot"]], 8, 256), ktiles(w_lo[u["slot"]], 8, 256)
                wait(pe, lo_done, n + 1 + pace.by(pace.units))
                for f in range(2):
                    fs = slice(P * f, P * f + P)
                    wait(pe, emptied[2 + f], u["round"] + pace.by(pace.rounds))
                    for b, k0, x_hi, x_lo, kt in ((4 + 2 * f, 2, sb_hi, sb_lo, 2), (5 + 2 * f, 4, ssm_hi, ssm_lo, 4), (2 + f, 0, sc_hi, sc_lo, 2)):
                        for k in range(kt):
                            ins = three_passes(bank[:, b, :], hi[:, k0 + k, fs], lo[:, k0 + k, fs], x_hi[:, k, :], x_lo[:, k, :],
                                               k == 0, k == kt - 1)
                    ins.then_inc(acc_full, 1)

            gate_unit(n_mg, STILL)
            pe.wait_ge(sq_done, 4)
            for g in range(2):
                for t in range(NT):
                    for c in (2 * g, 2 * g + 1):
                        q = NT * g + t
                        ins = pe.matmul(bank[:, 4, q:q + 1], z_t[:, c, P * t:P * t + P], ones[:, 0:1],
                                        start=(c % 2 == 0), stop=(c % 2 == 1))
            ins.then_inc(ss_ready, 1)
            gate_unit(n_mg + 1, STILL)
            pe.wait_ge(rr_diags, 1)
            for g in range(2):
                for t in range(NT):
                    ins = pe.matmul(bank[:, 4 + g, P * t:P * t + P], ones[:], rr_diag[:, NT * g + t, :], start=True, stop=True)
                ins.then_inc(rr_spread, 1)
            gate_unit(n_mg + 2, STILL)
            pe.wait_ge(sb_lo_done, 2)
            pe.wait_ge(sc_lo_done, 2)
            pe.wait_ge(ssm_lo_done, 4)
            branches(n_mg + 3, STILL)
            with pe.Fori(0, 3) as p:
                for g in range(3):
                    gate_unit(n_mg + 4 + g, merge_pace(p))
                branches(n_mg + 7, merge_pace(p))
            pe.wait_ge(m2_lo_done, KD)
            mod_gate(4)
            chunks(n_out2, m2_hi, m2_lo)
            turn(3, xn_2)
            f_pairs(n_up2, KF // 2, c=3)
            pe.wait_ge(act_lo_done, 2 * KF)
            mod_gate(5)
            down(n_dn2, 1)


INPUTS = [
    "x", "mix_pre_g", "w_in", "b_forget", "sgu_norm_g", "w_spatial", "b_spatial", "w_out", "mix_post_g",
    "ffn_pre_g", "w_gate", "w_up", "w_down", "ffn_post_g", "c_2", "mod_w_2", "mod_b_2", "g_pre_mix_2",
    "g_post_mix_2", "g_pre_ffn_2", "g_post_ffn_2", "w_in_2", "sc_conv_w_2", "ssm_conv_w_2", "ssm_conv_b_2",
    "ssm_dt_bias_2", "ssm_a_log_2", "ssm_d_2", "ssm_norm_w_2", "w_sc_out_2", "w_sb_out_2", "w_ssm_out_2",
    "w_o_2", "w_ffn_in_2", "w_ffn_out_2",
]


def kernel(**inputs):
    import concourse.bacc as bacc
    from concourse.bass_utils import run_bass_kernel_spmd

    nc = bacc.Bacc("TRN2", target_bir_lowering=False, num_devices=1)
    arrays, args = {}, {}
    for name in INPUTS:
        array = np.ascontiguousarray(inputs[name])
        arrays[f"in_{name}"] = array
        args[name] = nc.dram_tensor(f"in_{name}", array.shape, mybir.dt.from_np(array.dtype), kind="ExternalInput").ap()
    out = nc.dram_tensor("out_0", arrays["in_x"].shape, F32, kind="ExternalOutput").ap()
    build(nc, args, out)
    result = run_bass_kernel_spmd(nc, [arrays], core_ids=[0])
    return result.results[0]["out_0"]
```

```python
from contextlib import ExitStack

import numpy as np
import concourse.bass as bass
from concourse import mybir

F32 = mybir.dt.float32
F32R = mybir.dt.float32r
ALU = mybir.AluOpType
ACT = mybir.ActivationFunctionType
AX_X = mybir.AxisListType.X

P = 128
TOK = 512
NT = TOK // P
D = 1024
KD = D // P
FF = 2816
KF = FF // P
HEADS = 8
EPS = 1e-6
MASKED = -1e30
KB = 1024

U_COL, VS_COL, Q_COL, K_COL, VA_COL, GA_COL, GB_COL, F_COL = (D * n for n in range(8))
SC_COL, SBQ_COL, SBV_COL, Z_COL, XBC_COL, DT_COL, GATE_COL = 0, 768, 1280, 1536, 2048, 2816, 2824
SB_HEADS = 4
SSM_HD = 64
CONV_K, SHORT_K = 4, 3
PAD = CONV_K

STREAM = [
    ("q", "F", 4), ("k", "F", 4), ("va", "T", 4), ("gates", "F", 8), ("vs", "T", 4), ("u", "F", 4),
    ("out", "T", 4), ("up", "F", 22), ("down", "D", 12),
    ("sbqk", "F", 2), ("sbv", "V", 1), ("xbc", "F", 3), ("z", "F", 2), ("sc", "F", 3),
    ("merge", "B", 16), ("out2", "T", 4), ("up2", "F", 22), ("down2", "D", 12),
]


def lay_out_stream():
    units, first = [], {}
    raw = [0, 0]
    full = mid = half = 0
    for stage, kind, count in STREAM:
        first[stage] = len(units)
        for n in range(count):
            u = {"n": len(units), "slot": len(units) % 2, "round": half // 2, "half": half % 2, "kt": 4}
            raw[u["slot"]] += 48 if (kind == "B" and n % 4 == 3) else 32
            u["raw"] = raw[u["slot"]]
            banks = {"F": 2, "B": 2, "V": 4}.get(kind, 0)
            if kind == "T":
                banks = 4 if n % 2 else 0
            if kind == "D":
                banks = 4 if n % 6 == 5 else 0
                u["kt"] = 2 if n % 6 == 0 else 4
                u["k0"] = max(0, 4 * (n % 6) - 2)
            full += banks
            half += banks // 2
            mid += banks == 0
            u["used"] = ("full", full) if banks else ("mid", mid)
            u["full"] = full - banks
            units.append(u)
    return units, first


UNITS, FIRST = lay_out_stream()


class Pace:

    def __init__(self, turn=None, units=0, rounds=0, mids=0, raw=(0, 0)):
        self.turn, self.units, self.rounds, self.mids, self.raw = turn, units, rounds, mids, raw

    def by(self, per_turn):
        return 0 if self.turn is None else self.turn * per_turn


STILL = Pace()


def pair_pace(turn):
    return Pace(turn, units=2, rounds=1, raw=(32, 32))


def chunk_pace(turn):
    return Pace(turn, units=2, rounds=1, mids=1, raw=(32, 32))


def down_pace(turn):
    return Pace(turn, units=6, rounds=1, mids=5, raw=(96, 96))


def merge_pace(turn):
    slot_of_branch = (FIRST["merge"] + 3) % 2
    return Pace(turn, units=4, rounds=2, raw=(80, 64) if slot_of_branch == 0 else (64, 80))


def build(nc, a, out):
    with ExitStack() as ctx:
        base = 16512

        def at(name, kb, shape, dt=F32):
            return nc.alloc_sbuf_tensor_at(name, shape, dt, offset=base + int(kb * KB))

        def sem(name):
            return ctx.enter_context(nc.semaphore(name))

        raw = [at(f"raw{s}", 8 * s, [P, 2048]) for s in range(2)]
        w_hi = [at(f"w_hi{s}", 16 + 8 * s, [P, 2048], F32R) for s in range(2)]
        w_lo = [at(f"w_lo{s}", 32 + 8 * s, [P, 2048], F32R) for s in range(2)]
        h_hi = at("h_hi", 48, [P, KD, TOK], F32R)
        h_lo = at("h_lo", 64, [P, KD, TOK], F32R)
        y_down = at("y_down", 48, [P, NT, D])
        x_res = at("x_res", 80, [P, NT, D])
        v_att = at("v_att", 80, [P, NT, D])
        mrg_hi = at("mrg_hi", 80, [P, KD, TOK], F32R)
        A = 96
        x_in = at("x_in", A + 32, [P, NT, D])
        xn_1 = at("xn_1", A + 0, [P, NT, D])
        xn_2 = at("xn_2", A + 16, [P, NT, D])
        h_tmp = at("h_tmp", A + 48, [P, 2, TOK])
        q_t = at("q_t", A + 0, [P, HEADS, TOK])
        k_t = at("k_t", A + 16, [P, HEADS, TOK])
        v_sgu = at("v_sgu", A + 16, [P, NT, D])
        gates = at("gate_a", A + 32, [P, 2 * KD, TOK])
        u_act = at("u_act", A + 48, [P, 2, TOK])
        m_tmp = at("m_tmp", A + 52, [P, 2, TOK])
        prob = at("prob", A + 64, [P, 2, TOK])
        prob_t = at("prob_t", A + 68, [P, 2, TOK])
        c_rows = at("c_rows", A + 72, [64, TOK], F32R)
        w_sp = at("w_sp", A + 76, [P, HEADS, P])
        mrg_lo = at("mrg_lo", A + 64, [P, KD, TOK], F32R)
        w_sp_t = at("w_sp_t", A + 80, [P, HEADS, P])
        b_sp = at("b_sp", A + 84, [P, HEADS, P])
        y_out = at("y_out", A + 0, [P, NT, D])
        act_hi = at("act_hi", A + 0, [P, KF, TOK], F32R)
        act_lo = at("act_lo", A + 44, [P, KF, TOK], F32R)
        sb_hi = at("sb_hi", A + 0, [P, 2, TOK], F32R)
        sb_lo = at("sb_lo", A + 4, [P, 2, TOK], F32R)
        sc_hi = at("sc_hi", A + 8, [P, 2, TOK], F32R)
        sc_lo = at("sc_lo", A + 12, [P, 2, TOK], F32R)
        ssm_hi = at("ssm_hi", A + 16, [P, 4, TOK], F32R)
        ssm_lo = at("ssm_lo", A + 24, [P, 4, TOK], F32R)
        qk2 = at("qk2", A + 16, [P, 4, TOK])
        v2 = at("v2", A + 24, [P, NT, 256])
        sc_raw = at("sc_raw", A + 16, [P, 6, TOK + PAD])
        z_t = at("z_t", A + 32, [P, 4, TOK])
        y_ssm = at("y_ssm", A + 40, [P, 4, TOK])
        sp_hi = at("sp_hi", A + 8, [P, 1280], F32R)
        sp_lo = at("sp_lo", A + 40, [P, 1280], F32R)
        conv_tmp = at("conv_tmp", A + 13, [P, TOK])
        xs_t = at("xs_t", A + 48, [P, 6, TOK])
        sp_tmp = at("sp_tmp", A + 60, [P, 2, TOK])
        att = at("att", A + 64, [P, 2, TOK])
        xdt = at("xdt", A + 60, [P, NT, TOK])
        xbc_raw = at("xbc_raw", A + 68, [P, 6, TOK + PAD])
        cb = at("cb", A + 68, [P, 2, 1280])
        decay = at("decay", A + 78, [P, 2, TOK])
        g_ssd = at("g_ssd", A + 82, [P, 2, TOK])
        a_rows = at("a_rows", A + 86, [64, TOK], F32R)
        rr_diag = at("rr_diag", A + 68, [P, 2 * NT, P])
        m2_hi = at("m2_hi", A + 40, [P, KD, TOK], F32R)
        m2_lo = at("m2_lo", A + 56, [P, KD, TOK], F32R)
        sig = at("sig", A + 72, [P, 6, TOK])
        m2_tmp = at("m2_tmp", A + 84, [P, 2, TOK])
        M = 184
        ident_r = at("ident", M, [P, P], F32R)
        ident = ident_r[:].bitcast(F32)
        ones = at("ones", M + 0.5, [P, P])
        mask_qk = at("mask_qk", M + 1, [P, P], F32R)
        mask_st = at("mask_st", M + 1.5, [P, P], F32R)
        mask_strict = at("mask_strict", M + 2, [P, P], F32R)
        one_st = at("one_st", M + 2.5, [P, P])
        one_strict = at("one_strict", M + 3, [P, P])
        neg_suffix = at("neg_suffix", M + 3.5, [P, P], F32R)
        neg_ones = at("neg_ones", M + 4, [P, P], F32R)
        gain_row = at("gain_row", M + 4.5, [P, D])
        mod_acc = at("mod_acc", M + 8.5, [P, 2, 512])
        mod_raw = at("mod_raw", M + 12.5, [P, 2, 512])
        row_a = at("row_a", M + 16.5, [HEADS, TOK])
        row_b = at("row_b", M + 18.5, [HEADS, TOK])
        silu_t = at("silu_t", M + 16.5, [P, 2, TOK])
        S0 = M + 20.5
        places = [S0]

        def small(name, n, dt=F32, parts=P):
            t = at(name, places[0], [parts, n], dt)
            places[0] += (n * 4 + 31) // 32 * 32 / KB
            return t

        wf = small("wf", 64)
        wf_hi = small("wf_hi", 64, F32R)
        wf_lo = small("wf_lo", 64, F32R)
        wf2 = small("wf2", 64)
        wf2_hi = small("wf2_hi", 64, F32R)
        wf2_lo = small("wf2_lo", 64, F32R)
        gain_1 = small("gain_1", KD)
        gain_2 = small("gain_2", KD)
        gain_3 = small("gain_3", KD)
        gain_4 = small("gain_4", KD)
        sgu_g = small("sgu_g", KD)
        bias_f = small("bias_f", 1)
        bias_dt = small("bias_dt", 1)
        a_log = small("a_log", 1)
        a_neg = small("a_neg", 1)
        c_col = small("c_col", KD)
        c_silu = small("c_silu", KD)
        shift_col = [small(f"shift{n}", KD) for n in (1, 2)]
        conv_w = small("conv_w", 6 * CONV_K)
        conv_b = small("conv_b", 6)
        short_w = small("short_w", 2 * SHORT_K)
        d_col = small("d_col", 4)
        norm_w = small("norm_w", 4)
        head_sel = small("head_sel", HEADS, F32R, 64)
        zeros_st = small("zeros_st", 1, F32R)
        power = small("power", 1)
        bn6 = small("bn6", NT * 2 * 6)
        mean_var = small("mean_var", NT * 2)
        sq_y = small("sq_y", 2 * NT)
        sq_x = small("sq_x", 2 * NT)
        inv_rms = small("inv_rms", NT)
        neg_max = small("neg_max", 2)
        row_sum = small("row_sum", 2)
        row_inv = small("row_inv", 2)
        ms_ssm = small("ms_ssm", 2 * NT)
        rr_ssm = small("rr_ssm", 2 * NT)
        dt_col = small("dt_col", NT * HEADS)
        nacs_col = small("nacs_col", NT * HEADS)
        assert base + places[0] * KB <= 229344, places
        bank = ctx.enter_context(nc.psum_tensor("bank", [P, 8, 512], F32))

        def sems(*names):
            return [sem(n) for n in names]

        raw_in = sems("raw_in0", "raw_in1")
        hi_done, lo_done = sems("hi_done", "lo_done")
        acc_full, mid_used = sems("acc_full", "mid_used")
        emptied = sems(*(f"emptied{b}" for b in range(4)))
        dve_chain, act_chain, pool_chain = sems("dve_chain", "act_chain", "pool_chain")
        consts, small_in, gain_1_in, x_again, wf_split = sems("consts", "small_in", "gain_1_in", "x_again", "wf_split")
        x_loaded = sems(*(f"x_loaded{t}" for t in range(NT)))
        y_squared, x_squared, y_root, x_root, ln_root = sems("y_squared", "x_squared", "y_root", "x_root", "ln_root")
        xn_a_ready, xn_b_ready, tr_ready = sems("xn_a_ready", "xn_b_ready", "tr_ready")
        h_hi_done, h_lo_done, stats_done, var_ready = sems("h_hi_done", "h_lo_done", "stats_done", "var_ready")
        gain_in, x_added, stored = sems("gain_in", "x_added", "stored")
        c_ready, mod_zero, mod_b_in, mod_summed = sems("c_ready", "mod_zero", "mod_b_in", "mod_summed")
        mod_w_in = sems("mod_w_in0", "mod_w_in1")
        mod_read, mod_out = sems("mod_read", "mod_out")
        row_mm, row_lin, row_ln, row_ready, rows_turned, cols_ready = sems(
            "row_mm", "row_lin", "row_ln", "row_ready", "rows_turned", "cols_ready")
        rows_split = sem("rows_split")
        score_ready, max_ready, prob_ready, prob_scaled = sems("score_ready", "max_ready", "prob_ready", "prob_scaled")
        pt_ready, pt_copied, pv_done, head_out, gated_b = sems("pt_ready", "pt_copied", "pv_done", "head_out", "gated_b")
        wsp_tr, wsp_done, v_normed, sgu_ready = sems("wsp_tr", "wsp_done", "v_normed", "sgu_ready")
        merged, merged_hi, merged_lo = sems("merged", "merged_hi", "merged_lo")
        act_hi_done, act_lo_done = sems("act_hi_done", "act_lo_done")
        pads_zero, conv_even, conv_odd, silu_x, z_silu = sems("pads_zero", "conv_even", "conv_odd", "silu_x", "z_silu")
        z2_ready, ln_done, sp_ready, e_ready, att_ready, av_done, sb_hi_done, sb_lo_done = sems(
            "z2_ready", "ln_done", "sp_ready", "e_ready", "att_ready", "av_done", "sb_hi_done", "sb_lo_done")
        short_done, sc_hi_done, sc_lo_done = sems("short_done", "sc_hi_done", "sc_lo_done")
        xs_turned, xdt_done, cb_ready, cb_done = sems("xs_turned", "xdt_done", "cb_ready", "cb_done")
        dec_ready, dec_done, g_ready, ys_done, y_pair = sems("dec_ready", "dec_done", "g_ready", "ys_done", "y_pair")
        y_gated, sq_done, ss_ready, ms2_ready, rr_ready = sems("y_gated", "sq_done", "ss_ready", "ms2_ready", "rr_ready")
        rr_diags, rr_spread = sems("rr_diags", "rr_spread")
        y_normed, ssm_hi_done, ssm_lo_done = sems("y_normed", "ssm_hi_done", "ssm_lo_done")
        m2_ready, m2_hi_done, m2_lo_done = sems("m2_ready", "m2_hi_done", "m2_lo_done")

        def wait(eng, s, value):
            if not isinstance(value, int) or value > 0:
                eng.wait_ge(s, value)

        def wait_used(eng, n, pace=STILL):
            if n < 0:
                assert pace is STILL
                return
            kind, value = UNITS[n]["used"]
            if kind == "full":
                wait(eng, acc_full, value + pace.by(4 * pace.rounds))
            else:
                wait(eng, mid_used, value + pace.by(pace.mids))

        def wait_full(eng, n, b, pace=STILL):
            wait(eng, acc_full, UNITS[n]["full"] + b + 1 + pace.by(4 * pace.rounds))

        def wait_emptied(eng, n, b, pace=STILL):
            u = UNITS[n]
            wait(eng, emptied[2 * u["half"] + b], u["round"] + 1 + pace.by(pace.rounds))

        def ktiles(t, k, width):
            return t[:, :].rearrange("p (k c) -> p k c", c=width)[:, 0:k, :]

        class Chain:

            def __init__(self, eng, s):
                self.eng, self.sem, self.count, self.turn, self.each = eng, s, 0, None, 0

            def then(self, ins):
                self.count += 1
                ins.then_inc(self.sem, 1)
                self.wait()

            def wait(self):
                v = self.count if self.turn is None else self.count + self.turn * self.each
                self.eng.wait_ge(self.sem, v)

            def enter(self, turn, each):
                self.turn, self.each, self.first = turn, each, self.count

            def leave(self, turns):
                assert self.count - self.first == self.each
                self.count, self.turn = self.first + turns * self.each, None

        n_q, n_k, n_va, n_g, n_vs, n_u = (FIRST[s] for s in ("q", "k", "va", "gates", "vs", "u"))
        n_out, n_up, n_dn = FIRST["out"], FIRST["up"], FIRST["down"]
        n_qk2, n_v2, n_x, n_z, n_sc = (FIRST[s] for s in ("sbqk", "sbv", "xbc", "z", "sc"))
        n_mg, n_out2, n_up2, n_dn2 = FIRST["merge"], FIRST["out2"], FIRST["up2"], FIRST["down2"]
        WIDTH = [TOK - P * j for j in range(NT)]
        START = [sum(WIDTH[:j]) for j in range(NT)]
        ATT_TASKS = [(h, i) for h in range(HEADS) for i in range(NT)]
        SB_TASKS = [(h, j) for h in range(SB_HEADS) for j in reversed(range(NT))]
        SSD_TASKS = [(h, j) for h in range(HEADS) for j in range(NT)]
        SB_QUARTERS = [range(5 * s // 4, 5 * (s + 1) // 4) for s in range(len(SB_TASKS))]
        MOD_PAIRS = [(0, 1), (2, 3), (6, 7), (8, 9), (4, 5), (10, 11)]
        DVE_STEPS = ["m0 x0 m1 x1 m2 m3 n0 x2 n1 x3 n2 n3", "m0 x0 m1 x1 m2 x2 m3 x3 n0 n1 n2 n3",
                     "m0 x0 m1 x1 m2 n0 x2 m3 n1 x3 n2 n3", "m0 x0 m1 x1 m2 x2 m3 x3"]
        ACT_STEPS = ["q0 q1 s0 q2 n0 s1 q3 n1 s2 s3 n2 n3", "q0 q1 s0 q2 s1 q3 s2 n0 n1 s3 n2 n3",
                     "q0 q1 s0 q2 n0 s1 q3 n1 s2 s3 n2 n3", "q0 q1 q2 q3"]
        POOL_STEPS = ["p0 p1 r0 p2 r1 p3 r2 r3", "p0 p1 r0 p2 r1 p3 r2 r3", "p0 p1 r0 p2 r1 p3 r2 r3", "p0 p1 p2 p3"]

        def steps(order):
            return [(step[0], int(step[1])) for step in order.split()]

        HALVES = [slice(0, 512), slice(512, 1024)]
        POST_UNIT = [n_out + 3, n_dn + 11, n_out2 + 3, n_dn2 + 11]

        SMALL = 24

        block = ctx.enter_context(nc.Block())

        @block.sync
        def _(sp):
            def kview(name):
                return a[name][0].rearrange("(k p) n -> p k n", p=P)

            w_in, w_in2 = kview("w_in"), kview("w_in_2")

            def free(n, pace=STILL):
                wait(sp, lo_done, n - 1 + pace.by(pace.units))

            def load(n, dst, src):
                sp.dma_start(dst, src).then_inc(raw_in[UNITS[n]["slot"]], 16)

            def load_f(n, w, col, pace=STILL):
                free(n, pace)
                r = ktiles(raw[UNITS[n]["slot"]], 8, 256)
                for k in (0, 4):
                    load(n, r[:, k:k + 4, :], w[:, k:k + 4, bass.ds(col, 256)])

            def load_t(n, w, k0, col, pace):
                free(n, pace)
                kt = UNITS[n]["kt"]
                r = ktiles(raw[UNITS[n]["slot"]], kt, 512)
                for k in (0, kt // 2):
                    load(n, r[:, k:k + kt // 2, :], w[:, k0 + k:k0 + k + kt // 2, bass.ds(col, 512)])

            def stream_f(n0, w, col0, turns):
                with sp.Fori(0, turns) as i:
                    for j in range(2):
                        load_f(n0 + j, w, 512 * i + (col0 + 256 * j), pair_pace(i))

            def stream_t(n0, w, col0):
                with sp.Fori(0, 2) as c:
                    for j in range(2):
                        load_t(n0 + j, w, 4 * j, 512 * c + col0, chunk_pace(c))

            def stream_up(n0, wg, wu, up_col):
                with sp.Fori(0, KF // 2) as i:
                    for j in range(2):
                        free(n0 + j, pair_pace(i))
                        r = ktiles(raw[UNITS[n0 + j]["slot"]], 8, 256)
                        load(n0 + j, r[:, :, 0:P], wg[:, :, bass.ds(256 * i + P * j, P)])
                        load(n0 + j, r[:, :, P:2 * P], wu[:, :, bass.ds(256 * i + (up_col + P * j), P)])

            def stream_down(n0, w):
                with sp.Fori(0, 2) as c:
                    for j in range(6):
                        load_t(n0 + j, w, UNITS[n0 + j]["k0"], 512 * c, down_pace(c))

            def column(name):
                return a[name][0].rearrange("(k p) -> p k", p=P)

            def load_small():
                loads = [
                    (c_col[:], column("c_2")),
                    (wf[:, :].rearrange("p (k n) -> p k n", n=8), w_in[:, :, F_COL:F_COL + 8]),
                    (wf2[:, :].rearrange("p (k n) -> p k n", n=8), w_in2[:, :, DT_COL:DT_COL + 8]),
                    (gain_2[:], column("ffn_pre_g")), (gain_3[:], column("g_pre_mix_2")), (gain_4[:], column("g_pre_ffn_2")),
                    (sgu_g[:], column("sgu_norm_g")),
                    (bias_f[0:HEADS, :], a["b_forget"].rearrange("a h -> h a")),
                    (a_log[0:HEADS, :], a["ssm_a_log_2"].rearrange("a h -> h a")),
                    (bias_dt[0:HEADS, :], a["ssm_dt_bias_2"].rearrange("a h -> h a")),
                    (conv_b[:], column("ssm_conv_b_2")), (norm_w[:], column("ssm_norm_w_2")),
                    (w_sp[:], a["w_spatial"][0].rearrange("g t s -> t g s")),
                    (gain_row[:], a["mix_post_g"][0].partition_broadcast(P)),
                    (b_sp[:], a["b_spatial"][0].partition_broadcast(P)),
                ]
                for k in range(CONV_K):
                    loads.append((conv_w[:, 6 * k:6 * k + 6], a["ssm_conv_w_2"][0, k].rearrange("(c p) -> p c", p=P)))
                for k in range(SHORT_K):
                    loads.append((short_w[:, 2 * k:2 * k + 2], a["sc_conv_w_2"][0, k].rearrange("(c p) -> p c", p=P)))
                for half in range(2):
                    loads.append((d_col[64 * half:64 * half + 64, :],
                                  a["ssm_d_2"][0].rearrange("(t h) -> h t", h=2)[half].partition_broadcast(64)))
                assert len(loads) == SMALL
                with nc.allow_non_contiguous_dma(reason="a few thousand scalars, once"):
                    for dst, src in loads:
                        sp.dma_start(dst, src).then_inc(small_in, 16)

            def next_gain(name, k):
                wait_emptied(sp, POST_UNIT[k - 1], 3)
                sp.dma_start(gain_row[:], a[name][0].partition_broadcast(P)).then_inc(gain_in, 16)

            x_v = a["x"][0].rearrange("(t p) n -> p t n", p=P)
            load_f(n_q, w_in, Q_COL)
            for t in range(NT):
                sp.dma_start(x_in[:, t, :], x_v[:, t, :]).then_inc(x_loaded[t], 16)
            with nc.allow_non_contiguous_dma(reason="a few hundred scalars, once"):
                sp.dma_start(gain_1[:], column("mix_pre_g")).then_inc(gain_1_in, 16)
            load_f(n_q + 1, w_in, Q_COL + 256)
            load_small()
            for j in (2, 3):
                load_f(n_q + j, w_in, Q_COL + 256 * j)
            stream_f(n_k, w_in, K_COL, 2)
            stream_t(n_va, w_in, VA_COL)
            stream_f(n_g, w_in, GA_COL, 4)
            stream_t(n_vs, w_in, VS_COL)
            stream_f(n_u, w_in, U_COL, 2)
            stream_t(n_out, kview("w_out"), 0)
            sp.wait_ge(merged, KD)
            sp.dma_start(x_in[:], x_v).then_inc(x_again, 16)
            stream_up(n_up, kview("w_gate"), kview("w_up"), 0)
            next_gain("ffn_post_g", 1)
            stream_down(n_dn, kview("w_down"))
            for j in range(2):
                load_f(n_qk2 + j, w_in2, SBQ_COL + 256 * j)
            next_gain("g_post_mix_2", 2)
            load_f(n_v2, w_in2, SBV_COL)
            for j in range(3):
                load_f(n_x + j, w_in2, XBC_COL + 256 * j)
            for j in range(2):
                load_f(n_z + j, w_in2, Z_COL + 256 * j)
            for j in range(3):
                load_f(n_sc + j, w_in2, SC_COL + 256 * j)
            w_sc2, w_sb2, w_ssm2 = kview("w_sc_out_2"), kview("w_sb_out_2"), kview("w_ssm_out_2")
            for p in range(4):
                n = n_mg + 4 * p + 3
                for g in range(3):
                    load_f(n - 3 + g, w_in2, 256 * p + (GATE_COL + D * g))
                free(n)
                r = ktiles(raw[UNITS[n]["slot"]], 8, 256)
                load(n, r[:, 0:2, :], w_sc2[:, :, bass.ds(256 * p, 256)])
                load(n, r[:, 2:4, :], w_sb2[:, :, bass.ds(256 * p, 256)])
                load(n, r[:, 4:8, :], w_ssm2[:, :, bass.ds(256 * p, 256)])
            stream_t(n_out2, kview("w_o_2"), 0)
            w_ff2 = kview("w_ffn_in_2")
            stream_up(n_up2, w_ff2, w_ff2, FF)
            next_gain("g_post_ffn_2", 3)
            stream_down(n_dn2, kview("w_ffn_out_2"))
            out_v = out[0].rearrange("(t p) n -> t p n", p=P)
            for t in range(NT):
                sp.wait_ge(x_added, 8 * 3 + 2 * t + 2)
                sp.dma_start(out_v[t], x_res[:, t, :]).then_inc(stored, 16)
            sp.wait_ge(stored, 16 * NT)

        @block.gpsimd
        def _(gp):
            chain = Chain(gp, pool_chain)
            then = chain.then

            for t, keep, fill, step, mult, op in (
                    (ident_r, 1.0, 0.0, -1, 1, ALU.is_equal),
                    (mask_qk, 0.0, MASKED, -1, 1, ALU.is_ge),
                    (mask_st, 0.0, MASKED, 1, -1, ALU.is_ge),
                    (mask_strict, 0.0, MASKED, 1, -1, ALU.is_gt),
                    (one_st, 1.0, 0.0, 1, -1, ALU.is_ge),
                    (one_strict, 1.0, 0.0, 1, -1, ALU.is_gt),
                    (neg_suffix, -1.0, 0.0, -1, 1, ALU.is_ge)):
                then(gp.memset(mod_acc[:, 0, 0:P], keep))
                then(gp.affine_select(out=t[:], in_=mod_acc[:, 0, 0:P], compare_op=op, fill=fill, base=0,
                                      pattern=[[step, P]], channel_multiplier=mult))
            then(gp.tensor_tensor(head_sel[:], ident[0:64, 0:HEADS], ident[0:64, 32:32 + HEADS], ALU.add))
            then(gp.memset(ones[:], 1.0))
            then(gp.tensor_scalar(neg_ones[:], ones[:], -1.0, None, ALU.mult))
            then(gp.tensor_scalar(zeros_st[:], ones[:, 0:1], 0.0, None, ALU.mult))
            gp.memset(power[:], -0.5).then_inc(consts, 1)
            gp.wait_ge(consts, 1)

            def root(sq, t, ready):
                total = sq[:, t:t + 1]
                then(gp.tensor_scalar(total, total, sq[:, NT + t:NT + t + 1], EPS, ALU.add, ALU.add))
                gp.tensor_tensor(inv_rms[:, t:t + 1], total, power[:], ALU.pow).then_inc(ready, 1)

            def post_norm(k):
                for what, t in steps(POOL_STEPS[k]):
                    if what == "p":
                        gp.wait_ge(y_squared, 8 * k + NT + t + 1)
                        root(sq_y, t, y_root)
                    else:
                        gp.wait_ge(x_squared, 8 * (k + 1) + 2 * t + 2)
                        root(sq_x, t, x_root)

            mod_w = a["mod_w_2"][0].rearrange("(k p) n -> k p n", p=P)

            def mod_pair(pair):
                for which, chunk in enumerate(MOD_PAIRS[pair]):
                    m, col = 2 * pair + which, 512 * chunk
                    acc = mod_acc[:, which, :]
                    wait(gp, mod_read, pair)
                    gp.memset(acc, 0.0).then_inc(mod_zero, 1)
                    gp.wait_ge(mod_zero, m + 1)
                    gp.dma_start(mod_acc[0:1, which, :], a["mod_b_2"][:, col:col + 512]).then_inc(mod_b_in, 16)
                    for k in range(KD):
                        s, step = k % 2, KD * m + k
                        for ahead in ([0, 1] if k == 0 else [k + 1] if k + 1 < KD else []):
                            gp.dma_start(mod_raw[:, ahead % 2, :], mod_w[ahead, :, col:col + 512]).then_inc(mod_w_in[ahead % 2], 16)
                        gp.wait_ge(mod_w_in[s], 16 * (step // 2 + 1))
                        then(gp.tensor_scalar(mod_raw[:, s, :], mod_raw[:, s, :], c_silu[:, k:k + 1], None, ALU.mult))
                        if k == 0:
                            gp.wait_ge(mod_b_in, 16 * (m + 1))
                        ins = gp.tensor_tensor(acc, acc, mod_raw[:, s, :], ALU.add)
                        if k + 1 < KD:
                            then(ins)
                        else:
                            ins.then_inc(mod_summed, 1)
                            gp.wait_ge(mod_summed, m + 1)

            for t in range(NT):
                gp.wait_ge(x_squared, 2 * t + 2)
                root(sq_x, t, x_root)
            gp.wait_ge(c_ready, 1)
            mod_pair(0)
            for f in range(KD):
                wait_emptied(gp, n_g + 4 + f // 2, f % 2)
                then(gp.tensor_scalar(gates[:, KD + f, :], gates[:, KD + f, :], 1.0, None, ALU.add))
            for f in range(KD):
                gp.wait_ge(head_out, f + 1)
                gp.tensor_tensor(q_t[:, f, :], q_t[:, f, :], gates[:, KD + f, :], ALU.mult).then_inc(gated_b, 1)
            for t in range(NT):
                gp.wait_ge(var_ready, t + 1)
                var = mean_var[:, 2 * t + 1:2 * t + 2]
                then(gp.tensor_scalar(var, var, EPS, None, ALU.add))
                gp.tensor_tensor(inv_rms[:, t:t + 1], var, power[:], ALU.pow).then_inc(ln_root, 1)
            post_norm(0)
            mod_pair(1)
            mod_pair(2)
            post_norm(1)
            gp.wait_ge(pads_zero, 1)
            for c in (1, 3, 5):
                wait_emptied(gp, n_x + c // 2, 1)
                for k in reversed(range(CONV_K)):
                    o = PAD - (CONV_K - 1) + k
                    x, w = xbc_raw[:, c, o:o + TOK], conv_w[:, 6 * k + c:6 * k + c + 1]
                    if k == CONV_K - 1:
                        then(gp.tensor_scalar(xs_t[:, c, :], x, w, conv_b[:, c:c + 1], ALU.mult, ALU.add))
                        continue
                    then(gp.tensor_scalar(conv_tmp[:], x, w, None, ALU.mult))
                    ins = gp.tensor_tensor(xs_t[:, c, :], xs_t[:, c, :], conv_tmp[:], ALU.add)
                    if k > 0:
                        then(ins)
                    else:
                        ins.then_inc(conv_odd, 1)
                        gp.wait_ge(conv_odd, c // 2 + 1)
            mod_pair(3)
            for c in range(4):
                gp.wait_ge(y_gated, c + 1)
                gp.tensor_tensor(z_t[:, c, :], y_ssm[:, c, :], y_ssm[:, c, :], ALU.mult).then_inc(sq_done, 1)
            gp.wait_ge(ms2_ready, 1)
            gp.tensor_tensor(rr_ssm[:], ms_ssm[:], power[:, 0:1].to_broadcast([P, 2 * NT]), ALU.pow).then_inc(rr_ready, 1)
            mod_pair(4)
            post_norm(2)
            mod_pair(5)
            post_norm(3)

        @block.scalar
        def _(act):
            then = Chain(act, act_chain).then

            def split(n, pace=STILL, part=None):
                if n >= len(UNITS):
                    return
                u = UNITS[n]
                s, size = u["slot"], 512 * u["kt"]
                wait(act, raw_in[s], u["raw"] + pace.by(pace.raw[s]))
                wait_used(act, n - 2, pace)
                cols = slice(0, size) if part is None else slice(size // 2 * part, size // 2 * (part + 1))
                ins = act.copy(w_hi[s][:, cols], raw[s][:, cols])
                if part != 0:
                    ins.then_inc(hi_done, 1)

            def square(dst, src, where):
                return act.activation(dst, src, ACT.Square, scale=float(D) ** -0.5, accum_out=where)

            def norm_rows(c, x, xn, t):
                act.wait_ge(x_root, NT * c + t + 1)
                act.activation(xn[:, t, 0:512], x[:, t, 0:512], ACT.Copy, scale=inv_rms[:, t:t + 1]).then_inc(xn_a_ready, 1)

            def hi_parts(c, gain, shift):
                if shift is not None:
                    act.wait_ge(mod_out, 2 * c - 2)
                for k in range(KD):
                    act.wait_ge(tr_ready, KD * c + k + 1)
                    g = gain[:, k:k + 1]
                    if shift is None:
                        ins = act.activation(h_hi[:, k, :], bank[:, 4 + k % 4, :], ACT.Copy, scale=g)
                    elif k % 2 == 0:
                        ins = act.activation(h_hi[:, k, :], bank[:, 4 + k % 4, :], ACT.Identity, bias=shift[:, k:k + 1], scale=g)
                    else:
                        if k > 1:
                            act.wait_ge(h_lo_done, KD * c + k - 1)
                        then(act.activation(h_tmp[:, 1, :], bank[:, 4 + k % 4, :], ACT.Identity, bias=shift[:, k:k + 1], scale=g))
                        ins = act.copy(h_hi[:, k, :], h_tmp[:, 1, :])
                    ins.then_inc(h_hi_done, 1)

            def post_norm(k, n0, units, y, xn, gain, shift):
                def square_bank(c, t):
                    wait_full(act, n0 + units * c + units - 1, t)
                    square(y[:, t, HALVES[c]], bank[:, t, :], sq_y[:, NT * c + t:NT * c + t + 1]).then_inc(y_squared, 1)

                for j in range(units):
                    split(n0 + j + 1)
                for t in range(NT):
                    square_bank(0, t)
                for j in range(units):
                    split(n0 + units + j + 1)
                for what, t in steps(ACT_STEPS[k]):
                    if what == "q":
                        square_bank(1, t)
                    elif what == "s":
                        for half, cols in enumerate(HALVES):
                            act.wait_ge(x_added, 8 * k + 2 * t + half + 1)
                            square(y[:, t, cols], x_res[:, t, cols], sq_x[:, NT * half + t:NT * half + t + 1]).then_inc(x_squared, 1)
                    else:
                        if k == 1:
                            wait_full(act, POST_UNIT[1], 3)
                        norm_rows(k + 1, x_res, xn, t)
                if k < 3:
                    hi_parts(k + 1, gain, shift)

            def take(n, b, dst, pace=STILL, func=ACT.Copy, scale=1.0):
                wait_full(act, n, b, pace)
                act.activation(dst, bank[:, 2 * UNITS[n]["half"] + b, :], func, scale=scale).then_inc(
                    emptied[2 * UNITS[n]["half"] + b], 1)

            def chunks(n0, y, func=ACT.Copy):
                with act.Fori(0, 2) as c:
                    pace = chunk_pace(c)
                    for j in range(2):
                        split(n0 + j + 1, pace)
                    for t in range(NT):
                        take(n0 + 1, t, y[:, t, bass.ds(512 * c, 512)], pace, func)

            def hidden(n0, which):
                act.preload_act_table(ACT.Silu)
                with act.Fori(0, KF // 2) as i:
                    pace = pair_pace(i)
                    for j in range(2):
                        n = n0 + j
                        split(n + 1, pace)
                        take(n, 0, silu_t[:, j, :], pace, ACT.Silu)
                        wait_emptied(act, n, 1, pace)
                        act.copy(act_hi[:, bass.ds(2 * i + j, 1), :].rearrange("p a n -> p (a n)"),
                                 bank[:, 4 + j, :]).then_inc(act_hi_done, 1)

            def softplus_tail():
                rb = row_b[0:HEADS, :]
                then(act.activation(rb, row_a[0:HEADS, :], ACT.Abs))
                then(act.activation(rb, rb, ACT.Exp, scale=-1.0))
                act.activation(rb, rb, ACT.Ln, bias=1.0).then_inc(row_ln, 1)

            split(0)
            for t in range(NT):
                act.wait_ge(x_loaded[t], 16)
                for half, cols in enumerate(HALVES):
                    square(xn_1[:, t, cols], x_in[:, t, cols], sq_x[:, NT * half + t:NT * half + t + 1]).then_inc(x_squared, 1)
                if t > 0:
                    norm_rows(0, x_in, xn_1, t - 1)
            norm_rows(0, x_in, xn_1, NT - 1)
            act.wait_ge(gain_1_in, 16)
            hi_parts(0, gain_1, None)
            split(n_q + 1)
            act.wait_ge(small_in, 16 * SMALL)
            act.copy(wf_hi[:], wf[:]).then_inc(wf_split, 1)
            act.copy(wf2_hi[:], wf2[:]).then_inc(wf_split, 1)
            act.activation(c_silu[:], c_col[:], ACT.Silu).then_inc(c_ready, 1)
            act.preload_act_table_set("natural_log_exp_and_others")
            then(act.activation(a_neg[0:HEADS, :], a_log[0:HEADS, :], ACT.Exp))
            for j in range(4):
                if j > 0:
                    split(n_q + j + 1)
                take(n_q + j, 0, q_t[:, 2 * j, :], STILL, ACT.Copy, float(P) ** -0.5)
            with act.Fori(0, 2) as i:
                pace = pair_pace(i)
                for j in range(2):
                    split(n_k + j + 1, pace)
                    dst = k_t[:, bass.ds(4 * i + 2 * j, 1), :]
                    take(n_k + j, 0, dst.rearrange("p a n -> p (a n)"), pace)
            act.wait_ge(row_lin, 1)
            softplus_tail()
            chunks(n_va, v_att)
            for s, (h, i) in enumerate(ATT_TASKS):
                n, w = n_g + h, P * (i + 1)
                act.wait_ge(max_ready, s + 1)
                wait(act, pt_ready, s - 1)
                act.activation(prob[:, s % 2, 0:w], bank[:, 4 + s % 2, 0:w], ACT.Exp, bias=neg_max[:, s % 2:s % 2 + 1],
                               accum_out=row_sum[:, s % 2:s % 2 + 1]).then_inc(prob_ready, 1)
                if i == 0:
                    if h > 0:
                        take(n - 1, 1, gates[:, 2 * h - 1, :], STILL, ACT.Tanh, 0.5)
                if i < 2:
                    split(n + 1, part=i)
                if i == 2:
                    take(n, 0, gates[:, 2 * h, :], STILL, ACT.Tanh, 0.5)
            take(n_vs - 1, 1, gates[:, 2 * KD - 1, :], STILL, ACT.Tanh, 0.5)
            act.preload_act_table(ACT.Gelu_apprx_tanh)
            chunks(n_vs, v_sgu, ACT.Gelu_apprx_tanh)
            for f in range(KD):
                n = n_u + f // 2
                if f % 2 == 0:
                    split(n + 1)
                wait(act, merged, f - 1)
                if f == 0:
                    act.wait_ge(gated_b, KD)
                take(n, f % 2, u_act[:, f % 2, :], STILL, ACT.Gelu_apprx_tanh)
                act.wait_ge(merged, f + 1)
                act.activation(mrg_hi[:, f, :], m_tmp[:, f % 2, :], ACT.Copy, scale=0.5).then_inc(merged_hi, 1)
            post_norm(0, n_out, 2, y_out, xn_2, gain_2, None)
            hidden(n_up, 0)
            post_norm(1, n_dn, 6, y_down, xn_1, gain_3, shift_col[0])
            for j in range(2):
                split(n_qk2 + j + 1)
                take(n_qk2 + j, 0, qk2[:, 2 * j, :], STILL, ACT.Copy, SSM_HD ** -0.5 if j == 0 else 1.0)
            split(n_v2 + 1)
            for t in range(0, NT, 2):
                wait_full(act, n_v2, t)
                act.copy(v2[:, t, :], bank[:, t, 0:256]).then_inc(emptied[t], 1)
            act.preload_act_table_set("natural_log_exp_and_others")
            act.wait_ge(row_lin, 2)
            softplus_tail()
            split(n_x + 1)
            for s in range(len(SB_TASKS) + 1):
                last_quarters = SB_QUARTERS[s - 1] if s > 0 else []
                if s < len(SB_TASKS):
                    h, j = SB_TASKS[s]
                    w, z, t = WIDTH[j], bank[:, 4 + s % 2, :], sp_tmp[:, s % 2, :]
                    act.wait_ge(z2_ready, s + 1)
                    wait(act, sp_ready, s - 1)
                    then(act.activation(t[:, 0:w], z[:, 0:w], ACT.Abs))
                    then(act.activation(t[:, 0:w], t[:, 0:w], ACT.Exp, scale=-1.0))
                    act.activation(t[:, 0:w], t[:, 0:w], ACT.Ln, bias=1.0).then_inc(ln_done, 1)
                for q in last_quarters:
                    if q % 4 == 3:
                        split(n_x + q // 4 + 2, part=0)
                if s > 0:
                    w = WIDTH[SB_TASKS[s - 1][1]]
                    act.wait_ge(e_ready, s)
                    wait(act, av_done, s - 2)
                    act.activation(att[:, (s - 1) % 2, 0:w], bank[:, 4 + (s - 1) % 2, 0:w], ACT.Exp).then_inc(att_ready, 1)
                for q in last_quarters:
                    m = q // 4
                    if q % 4 == 1:
                        take(n_x + m, 0, xbc_raw[:, 2 * m, PAD:PAD + TOK] if m < 3 else z_t[:, 2 * m - 6, :])
                    if q % 4 == 3:
                        split(n_x + m + 2, part=1)
            for hp in range(2):
                act.wait_ge(av_done, 8 * (hp + 1))
                act.copy(sb_hi[:, hp, :], bank[:, 6 + hp, :]).then_inc(sb_hi_done, 1)
            act.preload_act_table(ACT.Silu)
            for c in range(6):
                act.wait_ge(conv_odd if c % 2 else conv_even, c // 2 + 1)
                act.activation(xs_t[:, c, :], xs_t[:, c, :], ACT.Silu).then_inc(silu_x, 1)
            for c in range(4):
                wait_emptied(act, n_z + c // 2, c % 2)
                act.activation(z_t[:, c, :], z_t[:, c, :], ACT.Silu).then_inc(z_silu, 1)
            take(n_sc, 0, sc_raw[:, 0, PAD:PAD + TOK])
            act.preload_act_table(ACT.Exp)
            for s in range(8):
                g, j = divmod(s, NT)
                act.wait_ge(cb_ready, s + 1)
                act.copy(cb[:, g, START[j]:START[j] + WIDTH[j]], bank[:, 4 + s % 4, 0:WIDTH[j]]).then_inc(cb_done, 1)
            for s, (h, j) in enumerate(SSD_TASKS):
                w = WIDTH[j]
                act.wait_ge(dec_ready, s + 1)
                wait(act, g_ready, s - 1)
                act.activation(decay[:, s % 2, 0:w], bank[:, 4 + s % 2, 0:w], ACT.Exp,
                               bias=nacs_col[:, HEADS * j + h:HEADS * j + h + 1]).then_inc(dec_done, 1)
                if s in (0, 1):
                    split(n_sc + 2, part=s)
                if s == 16:
                    take(n_sc + 1, 0, sc_raw[:, 2, PAD:PAD + TOK])
                if s in (17, 18):
                    split(n_mg, part=s - 17)
            take(n_sc + 2, 0, sc_raw[:, 4, PAD:PAD + TOK])
            act.preload_act_table(ACT.Sigmoid)

            def gate_pair(n, g, pace):
                for f in range(2):
                    take(n, f, sig[:, 2 * g + f, :], pace, ACT.Sigmoid)

            def merged_hi_parts(pair, p, pace):
                for f in range(2):
                    act.wait_ge(m2_ready, 2 * pair + f + 1 + pace.by(2))
                    act.copy(m2_hi[:, bass.ds(2 * p + (2 * pair + f), 1), :].rearrange("p a n -> p (a n)"),
                             m2_tmp[:, f, :]).then_inc(m2_hi_done, 1)

            split(n_mg + 1)
            gate_pair(n_mg, 0, STILL)
            for c in range(2):
                act.wait_ge(short_done, c + 1)
                act.copy(sc_hi[:, c, :], sc_raw[:, 4 + c, PAD:PAD + TOK]).then_inc(sc_hi_done, 1)
            split(n_mg + 2)
            gate_pair(n_mg + 1, 1, STILL)
            split(n_mg + 3)
            for c in range(4):
                act.wait_ge(y_normed, c + 1)
                act.copy(ssm_hi[:, c, :], y_ssm[:, c, :]).then_inc(ssm_hi_done, 1)
            gate_pair(n_mg + 2, 2, STILL)
            split(n_mg + 4)
            merged_hi_parts(0, 0, STILL)
            with act.Fori(0, 3) as p:
                pace = merge_pace(p)
                for g in range(3):
                    split(n_mg + 4 + g + 1, pace)
                    gate_pair(n_mg + 4 + g, g, pace)
                split(n_mg + 8, pace)
                merged_hi_parts(1, p, pace)
            post_norm(2, n_out2, 2, y_out, xn_2, gain_4, shift_col[1])
            hidden(n_up2, 1)
            post_norm(3, n_dn2, 6, y_down, None, None, None)

        @block.vector
        def _(dve):
            chain = Chain(dve, dve_chain)
            then = chain.then

            def split(n, pace=STILL, part=None):
                if n >= len(UNITS):
                    return
                u = UNITS[n]
                s, size = u["slot"], 512 * u["kt"]
                wait(dve, hi_done, n + 1 + pace.by(pace.units))
                cols = slice(0, size) if part is None else slice(size // 2 * part, size // 2 * (part + 1))
                ins = dve.tensor_tensor(w_lo[s][:, cols], raw[s][:, cols], w_hi[s][:, cols].bitcast(F32), ALU.subtract)
                if part != 0:
                    ins.then_inc(lo_done, 1)

            def take(n, b, dst, pace=STILL):
                wait_full(dve, n, b, pace)
                dve.tensor_copy(dst, bank[:, 2 * UNITS[n]["half"] + b, :]).then_inc(emptied[2 * UNITS[n]["half"] + b], 1)

            def norm_rows(c, x, xn, t):
                dve.wait_ge(x_root, NT * c + t + 1)
                dve.tensor_scalar(xn[:, t, 512:], x[:, t, 512:], inv_rms[:, t:t + 1], None, ALU.mult).then_inc(xn_b_ready, 1)

            def lo_parts(c, gain, shift):
                if shift is not None:
                    dve.wait_ge(mod_out, 2 * c - 2)
                for k in range(KD):
                    src = bank[:, 4 + k % 4, :]
                    dve.wait_ge(h_hi_done, KD * c + k + 1)
                    if shift is None:
                        dve.scalar_tensor_tensor(h_lo[:, k, :], src, gain[:, k:k + 1], h_hi[:, k, :].bitcast(F32),
                                                 ALU.mult, ALU.subtract).then_inc(h_lo_done, 1)
                    else:
                        if k % 2 == 0:
                            wait(dve, h_lo_done, KD * c + k - 1)
                            then(dve.tensor_scalar(h_tmp[:, 0, :], src, gain[:, k:k + 1], shift[:, k:k + 1], ALU.mult, ALU.add))
                        dve.tensor_tensor(h_lo[:, k, :], h_tmp[:, k % 2, :], h_hi[:, k, :].bitcast(F32),
                                          ALU.subtract).then_inc(h_lo_done, 1)

            def post_norm(k, n0, units, y, old, xn, gain, shift):
                def gain_bank(c, t):
                    dve.wait_ge(y_squared, 8 * k + NT * c + t + 1)
                    dve.tensor_tensor(y[:, t, HALVES[c]], bank[:, t, :], gain_row[:, HALVES[c]], ALU.mult).then_inc(emptied[t], 1)

                wait(dve, gain_in, 16 * k)
                for j in range(units):
                    split(n0 + j + 1)
                    if k >= 2 and j == 0:
                        mod_gate(k + 2, k, 4 if k == 2 else 6)
                        dve.wait_ge(mod_out, 3 + k)
                for t in range(NT):
                    gain_bank(0, t)
                for j in range(units):
                    split(n0 + units + j + 1)
                for what, t in steps(DVE_STEPS[k]):
                    if what == "m":
                        gain_bank(1, t)
                    elif what == "x":
                        if k == 0 and t == 0:
                            dve.wait_ge(x_again, 16)
                            wait_used(dve, POST_UNIT[0] - 1)
                        if k == 0 and t == 2:
                            wait_full(dve, POST_UNIT[0], 3)
                        wait_emptied(dve, POST_UNIT[k], t)
                        dve.wait_ge(y_root, NT * k + t + 1)
                        for cols in HALVES:
                            dve.scalar_tensor_tensor(x_res[:, t, cols], y[:, t, cols], inv_rms[:, t:t + 1], old[:, t, cols],
                                                     ALU.mult, ALU.add).then_inc(x_added, 1)
                    else:
                        if k == 1:
                            wait_full(dve, POST_UNIT[1], 3)
                        norm_rows(k + 1, x_res, xn, t)
                if k < 3:
                    lo_parts(k + 1, gain, shift)

            def chunks(n0, y):
                with dve.Fori(0, 2) as c:
                    pace = chunk_pace(c)
                    for j in range(2):
                        split(n0 + j + 1, pace)
                    if y is not None:
                        for t in range(NT):
                            wait_emptied(dve, n0 + 1, t, pace)
                            ins = dve.bn_stats(bn6[:, bass.ds(6 * c + 12 * t, 6)], y[:, t, bass.ds(512 * c, 512)])
                        ins.then_inc(stats_done, 1)

            def hidden(n0, which):
                with dve.Fori(0, KF // 2) as i:
                    pace = pair_pace(i)
                    for j in range(2):
                        n = n0 + j
                        split(n + 1, pace)
                        wait_emptied(dve, n, 0, pace)
                        wait_full(dve, n, 1, pace)
                        wait(dve, lo_done, n + 2 + pace.by(pace.units))
                        up = 2 * UNITS[n]["half"] + 1
                        dve.tensor_tensor(bank[:, 4 + j, :], bank[:, up, :], silu_t[:, j, :], ALU.mult).then_inc(emptied[up], 1)
                        dve.wait_ge(act_hi_done, KF * which + j + 1 + pace.by(2))
                        m = bass.ds(2 * i + j, 1)
                        dve.tensor_tensor(act_lo[:, m, :].rearrange("p a n -> p (a n)"), bank[:, 4 + j, :],
                                          act_hi[:, m, :].bitcast(F32).rearrange("p a n -> p (a n)"),
                                          ALU.subtract).then_inc(act_lo_done, 1)

            def mod_columns(pair, dst, scale):
                dve.wait_ge(mod_read, pair + 1)
                if scale:
                    ins = dve.scalar_tensor_tensor(dst[:], bank[:, 7, 0:KD], 1.0, dst[:], ALU.add, ALU.mult)
                else:
                    ins = dve.tensor_copy(dst[:], bank[:, 7, 0:KD])
                ins.then_inc(mod_out, 1)

            def mod_gate(pair, k, b):
                dve.wait_ge(gain_in, 16 * k)
                dve.wait_ge(mod_read, pair + 1)
                dve.tensor_tensor(gain_row[:, 0:512], gain_row[:, 0:512], bank[:, b, :], ALU.mult)
                dve.tensor_tensor(gain_row[:, 512:1024], gain_row[:, 512:1024], bank[:, b + 1, :], ALU.mult).then_inc(mod_out, 1)

            def split_rows(src, dst):
                then(dve.tensor_scalar(dst[:], h_hi[0:64, 0, :].bitcast(F32), 0.0, None, ALU.mult))
                then(dve.tensor_copy(dst[0:HEADS, :], src))
                dve.tensor_tensor(dst[32:32 + HEADS, :], src, dst[0:HEADS, :].bitcast(F32), ALU.subtract).then_inc(rows_split, 1)

            split(0)
            for t in range(NT):
                norm_rows(0, x_in, xn_1, t)
            dve.wait_ge(gain_1_in, 16)
            lo_parts(0, gain_1, None)
            dve.wait_ge(small_in, 16 * SMALL)
            dve.wait_ge(wf_split, 2)
            dve.tensor_tensor(wf_lo[:], wf[:], wf_hi[:].bitcast(F32), ALU.subtract)
            dve.tensor_tensor(wf2_lo[:], wf2[:], wf2_hi[:].bitcast(F32), ALU.subtract).then_inc(wf_split, 1)
            for n0, dst in ((n_q, q_t), (n_k, k_t)):
                with dve.Fori(0, 2) as i:
                    pace = pair_pace(i)
                    for j in range(2):
                        split(n0 + j + 1, pace)
                        d = dst[:, bass.ds(4 * i + (2 * j + 1), 1), :].rearrange("p a n -> p (a n)")
                        if n0 == n_q:
                            wait_full(dve, n0 + j, 1, pace)
                            b = 2 * UNITS[n0 + j]["half"] + 1
                            dve.tensor_scalar(d, bank[:, b, :], float(P) ** -0.5, None, ALU.mult).then_inc(emptied[b], 1)
                        else:
                            take(n0 + j, 1, d, pace)
            ra, rb = row_a[0:HEADS, :], row_b[0:HEADS, :]
            dve.wait_ge(row_mm, 1)
            dve.tensor_scalar(ra, bank[0:HEADS, 4, :], bias_f[0:HEADS, :], None, ALU.add).then_inc(row_lin, 1)
            dve.wait_ge(row_ln, 1)
            then(dve.scalar_tensor_tensor(ra, ra, 0.0, rb, ALU.min, ALU.subtract))
            then(dve.tensor_tensor_scan(rb, ra, ra, 0.0, ALU.add, ALU.bypass))
            then(dve.tensor_scalar(ra, rb, -1.0, None, ALU.mult))
            split_rows(ra, c_rows)
            chunks(n_va, None)
            for s in range(len(ATT_TASKS) + 3):
                if s >= 3 and ATT_TASKS[s - 3][1] == NT - 1:
                    dve.wait_ge(pv_done, s - 2)
                    dve.tensor_copy(q_t[:, ATT_TASKS[s - 3][0], :], bank[:, 7, :]).then_inc(head_out, 1)
                if s < len(ATT_TASKS):
                    h, i = ATT_TASKS[s]
                    w, b = P * (i + 1), s % 2
                    dve.wait_ge(score_ready, s + 1)
                    dve.tensor_reduce(neg_max[:, b:b + 1], bank[:, 4 + b, 0:w], AX_X, ALU.max, negate=True).then_inc(max_ready, 1)
                    dve.wait_ge(prob_ready, s + 1)
                    then(dve.reciprocal(row_inv[:, b:b + 1], row_sum[:, b:b + 1]))
                    dve.tensor_scalar(prob[:, b, 0:w], prob[:, b, 0:w], row_inv[:, b:b + 1], None, ALU.mult).then_inc(prob_scaled, 1)
                if 1 <= s <= len(ATT_TASKS):
                    w, b = P * (ATT_TASKS[s - 1][1] + 1), (s - 1) % 2
                    dve.wait_ge(pt_ready, s)
                    wait(dve, pv_done, s - 2)
                    dve.tensor_copy(prob_t[:, b, 0:w], bank[:, 6, 0:w]).then_inc(pt_copied, 1)
                if s < len(ATT_TASKS) and i in (1, 2):
                    split(n_g + h + 1, part=i - 1)
            mod_columns(0, shift_col[0], False)
            for g in range(0, HEADS, 4):
                dve.wait_ge(wsp_tr, g // 4 + 1)
                dve.tensor_tensor(w_sp_t[:, g:g + 4, :], bank[:, 4 + g // 4, :].rearrange("p (g t) -> p g t", t=P),
                                  one_st[:].unsqueeze(1).broadcast_to([P, 4, P]), ALU.mult).then_inc(wsp_done, 1)
            chunks(n_vs, v_sgu)
            split(n_u + 1)
            dve.wait_ge(stats_done, 2)
            for t in range(NT):
                dve.bn_aggr(mean_var[:, 2 * t:2 * t + 2], bn6[:, 12 * t:12 * t + 12]).then_inc(var_ready, 1)
            for t in range(NT):
                dve.wait_ge(ln_root, t + 1)
                dve.tensor_scalar(v_sgu[:, t, :], v_sgu[:, t, :], mean_var[:, 2 * t:2 * t + 1], inv_rms[:, t:t + 1],
                                  ALU.subtract, ALU.mult).then_inc(v_normed, 1)
            dve.wait_ge(gated_b, KD)
            for f in range(KD):
                n, m = n_u + f // 2, m_tmp[:, f % 2, :]
                if f % 2 == 0 and f > 0:
                    split(n + 1)
                dve.wait_ge(sgu_ready, f + 1)
                wait(dve, merged_hi, f - 1)
                then(dve.scalar_tensor_tensor(
                    m.rearrange("p (c t) -> p c t", t=P), bank[:, 4 + f % 2, :].rearrange("p (c t) -> p c t", t=P),
                    sgu_g[:, f:f + 1], b_sp[:, f, :].unsqueeze(1).broadcast_to([P, NT, P]), ALU.mult, ALU.add))
                wait_emptied(dve, n, f % 2)
                then(dve.tensor_tensor(m, m, u_act[:, f % 2, :], ALU.mult))
                then(dve.scalar_tensor_tensor(m, gates[:, f, :], 1.0, m, ALU.add, ALU.mult))
                dve.tensor_tensor(m, m, q_t[:, f, :], ALU.add).then_inc(merged, 1)
                dve.wait_ge(merged_hi, f + 1)
                dve.scalar_tensor_tensor(mrg_lo[:, f, :], m, 0.5, mrg_hi[:, f, :].bitcast(F32), ALU.mult,
                                         ALU.subtract).then_inc(merged_lo, 1)
            post_norm(0, n_out, 2, y_out, x_in, xn_2, gain_2, None)
            hidden(n_up, 0)
            mod_columns(1, gain_3, True)
            post_norm(1, n_dn, 6, y_down, x_res, xn_1, gain_3, shift_col[0])
            for j in range(2):
                split(n_qk2 + j + 1)
                if j == 0:
                    wait_full(dve, n_qk2, 1)
                    b = 2 * UNITS[n_qk2]["half"] + 1
                    dve.tensor_scalar(qk2[:, 1, :], bank[:, b, :], SSM_HD ** -0.5, None, ALU.mult).then_inc(emptied[b], 1)
                else:
                    take(n_qk2 + j, 1, qk2[:, 3, :])
            split(n_v2 + 1)
            for t in range(1, NT, 2):
                wait_full(dve, n_v2, t)
                dve.tensor_copy(v2[:, t, :], bank[:, t, 0:256]).then_inc(emptied[t], 1)
            mod_columns(2, shift_col[1], False)
            dve.memset(xbc_raw[:, :, 0:PAD], 0.0).then_inc(pads_zero, 1)
            dve.wait_ge(row_mm, 2)
            dve.tensor_scalar(ra, bank[0:HEADS, 4, :], bias_dt[0:HEADS, :], None, ALU.add).then_inc(row_lin, 1)
            dve.wait_ge(row_ln, 2)
            then(dve.scalar_tensor_tensor(ra, ra, 0.0, rb, ALU.max, ALU.add))
            then(dve.tensor_scalar(rb, ra, a_neg[0:HEADS, :], -1.0, ALU.mult, ALU.mult))
            dve.tensor_tensor_scan(rb, rb, rb, 0.0, ALU.add, ALU.bypass).then_inc(row_ready, 1)
            split(n_x + 1)
            dve.wait_ge(pads_zero, 1)

            def convolve(c, k):
                o = PAD - (CONV_K - 1) + k
                x, w, out_c = xbc_raw[:, c, o:o + TOK], conv_w[:, 6 * k + c:6 * k + c + 1], xs_t[:, c, :]
                if k == CONV_K - 1:
                    wait_emptied(dve, n_x + c // 2, 0)
                    then(dve.tensor_scalar(out_c, x, w, conv_b[:, c:c + 1], ALU.mult, ALU.add))
                elif k > 0:
                    then(dve.scalar_tensor_tensor(out_c, x, w, out_c, ALU.mult, ALU.add))
                else:
                    dve.scalar_tensor_tensor(out_c, x, w, out_c, ALU.mult, ALU.add).then_inc(conv_even, 1)

            for s in range(len(SB_TASKS) + 2):
                if s < len(SB_TASKS):
                    h, j = SB_TASKS[s]
                    w, lo, z = WIDTH[j], START[j], bank[:, 4 + s % 2, :]
                    dve.wait_ge(ln_done, s + 1)
                    wait(dve, e_ready, NT * h)
                    sp, j_cols = sp_tmp[:, s % 2, 0:w], slice(lo, lo + w)
                    then(dve.scalar_tensor_tensor(sp, z[:, 0:w], 0.0, sp, ALU.max, ALU.add))
                    then(dve.tensor_tensor(sp[:, 0:P], sp[:, 0:P], one_strict[:], ALU.mult))
                    then(dve.tensor_copy(sp_hi[:, j_cols], sp))
                    dve.tensor_tensor(sp_lo[:, j_cols], sp, sp_hi[:, j_cols].bitcast(F32), ALU.subtract).then_inc(sp_ready, 1)
                if 3 <= s < 15:
                    convolve(2 * ((s - 3) // CONV_K), CONV_K - 1 - (s - 3) % CONV_K)
                for q in SB_QUARTERS[s - 2] if s > 1 else []:
                    if q % 4 == 3:
                        split(n_x + q // 4 + 2, part=1)
                for q in SB_QUARTERS[s - 1] if 0 < s <= len(SB_TASKS) else []:
                    m = q // 4
                    if q % 4 == 3:
                        take(n_x + m, 1, xbc_raw[:, 2 * m + 1, PAD:PAD + TOK] if m < 3 else z_t[:, 2 * m - 5, :])
                        split(n_x + m + 2, part=0)
            for hp in range(2):
                dve.wait_ge(sb_hi_done, hp + 1)
                dve.tensor_tensor(sb_lo[:, hp, :], bank[:, 6 + hp, :], sb_hi[:, hp, :].bitcast(F32), ALU.subtract).then_inc(sb_lo_done, 1)
            dve.wait_ge(rows_turned, 1)
            dve.tensor_copy(dt_col[:], bank[:, 5, 0:NT * HEADS])
            dve.tensor_scalar(nacs_col[:], bank[:, 5, NT * HEADS:2 * NT * HEADS], -1.0, None, ALU.mult).then_inc(cols_ready, 1)
            dve.wait_ge(av_done, len(SB_TASKS))
            dve.memset(sc_raw[:, 2:4, 0:PAD], 0.0).then_inc(pads_zero, 1)
            for j in range(NT):
                dve.wait_ge(xs_turned, j + 1)
                dve.tensor_tensor(xdt[:, j, :].rearrange("p (h d) -> p h d", d=SSM_HD),
                                  bank[:, 4 + j, :].rearrange("p (h d) -> p h d", d=SSM_HD),
                                  dt_col[:, HEADS * j:HEADS * j + HEADS].unsqueeze(2).broadcast_to([P, HEADS, SSM_HD]),
                                  ALU.mult).then_inc(xdt_done, 1)
            take(n_sc, 1, sc_raw[:, 1, PAD:PAD + TOK])
            dve.wait_ge(row_ready, 1)
            split_rows(rb, a_rows)

            def gate_z(c):
                dve.wait_ge(z_silu, c + 1)
                dve.wait_ge(y_pair, c + 1)
                dve.tensor_tensor(y_ssm[:, c, :], y_ssm[:, c, :], z_t[:, c, :], ALU.mult).then_inc(y_gated, 1)

            for s, (h, j) in enumerate(SSD_TASKS):
                w, g = WIDTH[j], h // 4
                dve.wait_ge(dec_done, s + 1)
                if s == 0:
                    dve.wait_ge(cb_done, 8)
                wait(dve, ys_done, s - 1)
                dve.tensor_tensor(g_ssd[:, s % 2, 0:w], decay[:, s % 2, 0:w], cb[:, g, START[j]:START[j] + w],
                                  ALU.mult).then_inc(g_ready, 1)
                if s in (0, 1):
                    split(n_sc + 2, part=s)
                if s == 16:
                    take(n_sc + 1, 1, sc_raw[:, 3, PAD:PAD + TOK])
                if s in (17, 18):
                    split(n_mg, part=s - 17)
                if s % 8 == 2 and s > 8:
                    finish_pair = (s - 8) // 8
                    dve.wait_ge(ys_done, 8 * (finish_pair + 1))
                    dve.scalar_tensor_tensor(y_ssm[:, finish_pair, :], xs_t[:, finish_pair, :], d_col[:, finish_pair:finish_pair + 1],
                                             bank[:, 6 + finish_pair % 2, :], ALU.mult, ALU.add).then_inc(y_pair, 1)
                    gate_z(finish_pair)
            dve.wait_ge(ys_done, len(SSD_TASKS))
            dve.scalar_tensor_tensor(y_ssm[:, 3, :], xs_t[:, 3, :], d_col[:, 3:4], bank[:, 7, :], ALU.mult, ALU.add).then_inc(y_pair, 1)
            gate_z(3)
            take(n_sc + 2, 1, sc_raw[:, 5, PAD:PAD + TOK])
            split(n_mg + 1)
            wait_emptied(dve, n_sc + 1, 0)
            wait_emptied(dve, n_sc + 1, 1)
            wait_emptied(dve, n_sc + 2, 0)
            wait_emptied(dve, n_sc + 2, 1)
            wait_emptied(dve, n_sc, 0)
            wait_emptied(dve, n_sc, 1)
            for c in range(2):
                p_, o_ = sc_raw[:, 2 + c, :], sc_raw[:, 4 + c, PAD:PAD + TOK]
                then(dve.tensor_tensor(p_[:, PAD:PAD + TOK], p_[:, PAD:PAD + TOK], o_, ALU.mult))
                then(dve.tensor_scalar(o_, p_[:, PAD:PAD + TOK], short_w[:, 4 + c:5 + c], None, ALU.mult))
                then(dve.scalar_tensor_tensor(o_, p_[:, PAD - 1:PAD - 1 + TOK], short_w[:, 2 + c:3 + c], o_, ALU.mult, ALU.add))
                then(dve.scalar_tensor_tensor(o_, p_[:, PAD - 2:PAD - 2 + TOK], short_w[:, c:c + 1], o_, ALU.mult, ALU.add))
                dve.tensor_tensor(o_, o_, sc_raw[:, c, PAD:PAD + TOK], ALU.mult).then_inc(short_done, 1)
            for c in range(2):
                dve.wait_ge(sc_hi_done, c + 1)
                dve.tensor_tensor(sc_lo[:, c, :], sc_raw[:, 4 + c, PAD:PAD + TOK], sc_hi[:, c, :].bitcast(F32), ALU.subtract).then_inc(sc_lo_done, 1)
            dve.wait_ge(ss_ready, 1)
            dve.tensor_scalar(ms_ssm[:], bank[:, 4, 0:2 * NT], 1.0 / 256, EPS, ALU.mult, ALU.add).then_inc(ms2_ready, 1)
            split(n_mg + 2)
            dve.wait_ge(rr_ready, 1)
            for q in range(2 * NT):
                ins = dve.tensor_scalar(rr_diag[:, q, :], ident[:], rr_ssm[:, q:q + 1], None, ALU.mult)
            ins.then_inc(rr_diags, 1)
            mod_columns(3, gain_4, True)
            split(n_mg + 3)
            for c in range(4):
                dve.wait_ge(rr_spread, c // 2 + 1)
                dve.scalar_tensor_tensor(y_ssm[:, c, :], y_ssm[:, c, :], norm_w[:, c:c + 1], bank[:, 4 + c // 2, :],
                                         ALU.mult, ALU.mult).then_inc(y_normed, 1)
            for c in range(4):
                dve.wait_ge(ssm_hi_done, c + 1)
                dve.tensor_tensor(ssm_lo[:, c, :], y_ssm[:, c, :], ssm_hi[:, c, :].bitcast(F32), ALU.subtract).then_inc(ssm_lo_done, 1)
            def merge(n, pair, p, pace):
                for g in range(3):
                    for f in range(2):
                        wait_emptied(dve, n + g, f, pace)
                for f in range(2):
                    m = m2_tmp[:, f, :]
                    ga, gb, gc = (sig[:, 2 * g + f, :] for g in range(3))
                    wait_full(dve, n + 3, f, pace)
                    then(dve.tensor_tensor(m, gb, bank[:, 4 + 2 * f, :], ALU.mult))
                    then(dve.tensor_tensor(gc, gc, bank[:, 5 + 2 * f, :], ALU.mult))
                    then(dve.tensor_tensor(m, m, gc, ALU.add))
                    dve.tensor_tensor(ga, ga, bank[:, 2 + f, :], ALU.mult).then_inc(emptied[2 + f], 1)
                    wait_emptied(dve, n + 3, f, pace)
                    dve.tensor_tensor(m, m, ga, ALU.add).then_inc(m2_ready, 1)
                for f in range(2):
                    dve.wait_ge(m2_hi_done, 2 * pair + f + 1 + pace.by(2))
                    t = bass.ds(2 * p + (2 * pair + f), 1)
                    dve.tensor_tensor(m2_lo[:, t, :].rearrange("p a n -> p (a n)"), m2_tmp[:, f, :],
                                      m2_hi[:, t, :].bitcast(F32).rearrange("p a n -> p (a n)"), ALU.subtract).then_inc(m2_lo_done, 1)

            split(n_mg + 4)
            merge(n_mg, 0, 0, STILL)
            with dve.Fori(0, 3) as p:
                pace = merge_pace(p)
                chain.enter(p, 6)
                for g in range(4):
                    split(n_mg + 4 + g + 1, pace)
                merge(n_mg + 4, 1, p, pace)
            chain.leave(3)
            post_norm(2, n_out2, 2, y_out, x_res, xn_2, gain_4, shift_col[1])
            hidden(n_up2, 1)
            post_norm(3, n_dn2, 6, y_down, x_res, None, None, None)

        @block.tensor
        def _(pe):
            def three_passes(o, st_hi, st_lo, mv_hi, mv_lo, first, last):
                pe.matmul(o, st_hi, mv_hi, start=first, stop=False)
                pe.matmul(o, st_hi, mv_lo, start=False, stop=False)
                return pe.matmul(o, st_lo, mv_hi, start=False, stop=last)

            def feature_part(n, f, k):
                u = UNITS[n]
                hi, lo = ktiles(w_hi[u["slot"]], 8, 256), ktiles(w_lo[u["slot"]], 8, 256)
                fs = slice(P * f, P * f + P)
                ins = three_passes(bank[:, 2 * u["half"] + f, :], hi[:, k, fs], lo[:, k, fs], h_hi[:, k, :], h_lo[:, k, :],
                                   k == 0, k == KD - 1)
                if k == KD - 1:
                    ins.then_inc(acc_full, 1)

            def feature_tile(n, f, pace=STILL, ks=range(KD)):
                u = UNITS[n]
                if ks[0] == 0:
                    wait(pe, lo_done, n + 1 + pace.by(pace.units))
                    wait(pe, emptied[2 * u["half"] + f], u["round"] + pace.by(pace.rounds))
                for k in ks:
                    feature_part(n, f, k)

            def quarter(n, q):
                feature_tile(n, q // 2, ks=range(4 * (q % 2), 4 * (q % 2) + 4))

            def f_pairs(n0, turns, c=None, xn=None):
                if c is not None:
                    first_tile(c, xn, n0)
                    feature_tile(n0, 1)
                    for f in range(2):
                        feature_tile(n0 + 1, f)
                    n0, turns = n0 + 2, turns - 1
                with pe.Fori(0, turns) as i:
                    for j in range(2):
                        for f in range(2):
                            feature_tile(n0 + j, f, pair_pace(i))

            def token_unit(n, x_hi, x_lo, k0, first, last, pace, width=512):
                u = UNITS[n]
                kt = 8 if width == 256 else u["kt"]
                hi, lo = ktiles(w_hi[u["slot"]], kt, width), ktiles(w_lo[u["slot"]], kt, width)
                wait(pe, lo_done, n + 1 + pace.by(pace.units))
                for t in range(NT):
                    ts = slice(P * t, P * t + P)
                    if first:
                        wait(pe, emptied[t], u["round"] + pace.by(pace.rounds))
                    for k in range(kt):
                        ins = three_passes(bank[:, t, 0:width], x_hi[:, k0 + k, ts], x_lo[:, k0 + k, ts],
                                           hi[:, k, :], lo[:, k, :], first and k == 0, last and k == kt - 1)
                    if last:
                        ins.then_inc(acc_full, 1)
                if not last:
                    ins.then_inc(mid_used, 1)

            def chunks(n0, x_hi, x_lo, there=None):
                with pe.Fori(0, 2) as c:
                    for j in range(2):
                        if there is not None:
                            pe.wait_ge(there, 4 * j + 4)
                        token_unit(n0 + j, x_hi, x_lo, 4 * j, j == 0, j == 1, chunk_pace(c))

            def down(n0, which):
                with pe.Fori(0, 2) as c:
                    for j in range(6):
                        u = UNITS[n0 + j]
                        pe.wait_ge(act_lo_done, KF * which + u["k0"] + u["kt"])
                        token_unit(n0 + j, act_hi, act_lo, u["k0"], j == 0, j == 5, down_pace(c))

            def turn_ktile(xn, k):
                for t in range(NT):
                    ins = pe.transpose(bank[:, 4 + k % 4, P * t:P * t + P], xn[:, t, P * k:P * k + P], ident[:])
                ins.then_inc(tr_ready, 1)

            def first_tile(c, xn, n):
                for t in range(NT):
                    pe.wait_ge(xn_a_ready, NT * c + t + 1)
                    for k in range(4):
                        ins = pe.transpose(bank[:, 4 + k, P * t:P * t + P], xn[:, t, P * k:P * k + P], ident[:])
                        if t == NT - 1:
                            ins.then_inc(tr_ready, 1)
                wait(pe, lo_done, n + 1)
                wait(pe, emptied[2 * UNITS[n]["half"]], UNITS[n]["round"])
                pe.wait_ge(xn_b_ready, NT * c + NT)
                for k in range(KD):
                    pe.wait_ge(h_lo_done, KD * c + k + 1)
                    feature_part(n, 0, k)
                    if k < 4:
                        turn_ktile(xn, k + 4)

            def narrow(hi, lo):
                for k in range(KD):
                    ks = slice(8 * k, 8 * k + 8)
                    ins = three_passes(bank[0:HEADS, 4, :], hi[:, ks], lo[:, ks], h_hi[:, k, :], h_lo[:, k, :],
                                       k == 0, k == KD - 1)
                ins.then_inc(row_mm, 1)

            def mod_columns(pair):
                pe.wait_ge(mod_summed, 2 * pair + 2)
                for q in range(KD):
                    ins = pe.matmul(bank[:, 7, q:q + 1], mod_acc[:, q // 4, P * (q % 4):P * (q % 4) + P], ones[:, 0:1],
                                    start=True, stop=True)
                ins.then_inc(mod_read, 1)

            def mod_gate(pair, b):
                pe.wait_ge(mod_summed, 2 * pair + 2)
                for w in range(2):
                    ins = pe.matmul(bank[:, b + w, :], ones[:], mod_acc[:, w, :], start=True, stop=True)
                ins.then_inc(mod_read, 1)

            def head_row(h):
                return head_sel[:, h:h + 1].to_broadcast([64, P])

            pe.wait_ge(consts, 1)
            f_pairs(n_q, 2, c=0, xn=xn_1)
            f_pairs(n_k, 2)
            pe.wait_ge(wf_split, 3)
            narrow(wf_hi, wf_lo)
            chunks(n_va, h_hi, h_lo)
            for f in range(2):
                for n in (n_q + 2, n_q + 3, n_k + 2, n_k + 3):
                    wait_emptied(pe, n, f)
            for t in range(NT):
                wait_emptied(pe, n_va + 3, t)
            pe.wait_ge(rows_split, 1)
            for s in range(len(ATT_TASKS) + 2):
                if s < len(ATT_TASKS):
                    h, i = ATT_TASKS[s]
                    w, b = P * (i + 1), 4 + s % 2
                    wait(pe, prob_ready, s - 1)
                    pe.matmul(bank[:, b, 0:w], head_row(h), c_rows[:, 0:w], start=True, stop=False)
                    pe.matmul(bank[:, b, P * i:w], ident_r[:], mask_qk[:], start=False, stop=False)
                    pe.matmul(bank[:, b, 0:w], q_t[:, h, P * i:P * i + P], k_t[:, h, 0:w],
                              start=False, stop=True).then_inc(score_ready, 1)
                    quarter(n_g + h, i)
                if 1 <= s <= len(ATT_TASKS):
                    i, b = ATT_TASKS[s - 1][1], (s - 1) % 2
                    pe.wait_ge(prob_scaled, s)
                    wait(pe, pt_copied, s - 1)
                    for j in range(i + 1):
                        ins = pe.transpose(bank[:, 6, P * j:P * j + P], prob[:, b, P * j:P * j + P], ident[:])
                    ins.then_inc(pt_ready, 1)
                if s >= 2:
                    (h, i), b = ATT_TASKS[s - 2], (s - 2) % 2
                    pe.wait_ge(pt_copied, s - 1)
                    if i == 0:
                        wait(pe, head_out, h)
                    for j in range(i + 1):
                        ins = pe.matmul(bank[:, 7, P * i:P * i + P], v_att[:, j, P * h:P * h + P],
                                        prob_t[:, b, P * j:P * j + P], start=(j == 0), stop=(j == i))
                    ins.then_inc(pv_done, 1)
            pe.wait_ge(head_out, HEADS)
            mod_columns(0)
            pe.wait_ge(small_in, 16 * SMALL)
            for g in range(HEADS):
                ins = pe.transpose(bank[:, 4 + g // 4, P * (g % 4):P * (g % 4) + P], w_sp[:, g, :], ident[:])
                if g % 4 == 3:
                    ins.then_inc(wsp_tr, 1)
            chunks(n_vs, h_hi, h_lo)
            for f in range(KD):
                feature_tile(n_u + f // 2, f % 2)
                if f % 2 == 1:
                    pe.wait_ge(v_normed, NT)
                    pe.wait_ge(wsp_done, 2)
                    for g in (f - 1, f):
                        wait(pe, merged, g - 1)
                        for c in range(NT):
                            ins = pe.matmul(bank[:, 4 + g % 2, P * c:P * c + P], v_sgu[:, c, P * g:P * g + P], w_sp_t[:, g, :],
                                            start=True, stop=True)
                        ins.then_inc(sgu_ready, 1)
            chunks(n_out, mrg_hi, mrg_lo, there=merged_lo)
            f_pairs(n_up, KF // 2, c=1, xn=xn_2)
            mod_columns(1)
            down(n_dn, 0)
            first_tile(2, xn_1, n_qk2)
            feature_tile(n_qk2, 1)
            for f in range(2):
                feature_tile(n_qk2 + 1, f)
            narrow(wf2_hi, wf2_lo)
            token_unit(n_v2, h_hi, h_lo, 0, True, True, STILL, 256)
            mod_columns(2)
            pe.wait_ge(row_lin, 2)
            for f in range(2):
                wait_emptied(pe, n_qk2, f)
                wait_emptied(pe, n_qk2 + 1, f)
            for t in range(NT):
                wait_emptied(pe, n_v2, t)
            def eighth(r):
                feature_tile(n_x + r // 8, (r // 4) % 2, ks=range(2 * (r % 4), 2 * (r % 4) + 2))

            for s in range(len(SB_TASKS) + 2):
                if s < len(SB_TASKS):
                    h, j = SB_TASKS[s]
                    rows, w = slice(SSM_HD * (h % 2), SSM_HD * (h % 2) + SSM_HD), WIDTH[j]
                    wait(pe, att_ready, s - 1)
                    pe.matmul(bank[:, 4 + s % 2, 0:w], qk2[rows, 2 + h // 2, P * j:P * j + P], qk2[rows, h // 2, P * j:TOK],
                              start=True, stop=True).then_inc(z2_ready, 1)
                    eighth(5 * s // 2)
                if 1 <= s <= len(SB_TASKS):
                    (h, j), o = SB_TASKS[s - 1], bank[:, 4 + (s - 1) % 2, :]
                    w = WIDTH[j]
                    pe.wait_ge(sp_ready, s)
                    pe.matmul(o[:, 0:P], ident_r[:], mask_strict[:], start=False, stop=False, skip_group_check=True)
                    for j2 in range(j + 1, NT):
                        for sp in (sp_hi, sp_lo):
                            pe.matmul(o[:, P * (j2 - j):w], neg_ones[:], sp[:, START[j2]:START[j2] + WIDTH[j2]],
                                      start=False, stop=False, skip_group_check=True)
                    for sp in (sp_hi, sp_lo):
                        ins = pe.matmul(o[:, 0:w], neg_suffix[:], sp[:, START[j]:START[j] + w], start=False, stop=sp is sp_lo,
                                        skip_group_check=True)
                    ins.then_inc(e_ready, 1)
                if s < len(SB_TASKS):
                    eighth(5 * s // 2 + 1)
                if s >= 2:
                    h, j = SB_TASKS[s - 2]
                    pe.wait_ge(att_ready, s - 1)
                    rows = slice(SSM_HD * (h % 2), SSM_HD * (h % 2) + SSM_HD)
                    if j == NT - 1 and h % 2 == 0:
                        pe.matmul(bank[:, 6 + h // 2, :], zeros_st[:].to_broadcast([P, P]), h_hi[:, 0, :], start=True, stop=False)
                    pe.matmul(bank[rows, 6 + h // 2, P * j:TOK], v2[:, j, SSM_HD * h:SSM_HD * h + SSM_HD], att[:, s % 2, 0:WIDTH[j]],
                              start=False, stop=(j == 0)).then_inc(av_done, 1)
                if s < len(SB_TASKS):
                    for r in range(5 * s // 2 + 2, 5 * (s + 1) // 2):
                        eighth(r)
            pe.wait_ge(row_ready, 1)
            for r, row in ((0, row_a), (1, row_b)):
                for j in range(NT):
                    o = HEADS * (NT * r + j)
                    ins = pe.transpose(bank[:, 5, o:o + HEADS], row[0:HEADS, P * j:P * j + P], ident[0:HEADS, 0:HEADS])
            ins.then_inc(rows_turned, 1)
            feature_tile(n_sc, 0)
            pe.wait_ge(sb_lo_done, 2)
            feature_tile(n_sc, 1)
            pe.wait_ge(silu_x, 6)
            pe.wait_ge(cols_ready, 1)
            for j in range(NT):
                for c in range(4):
                    ins = pe.transpose(bank[:, 4 + j, P * c:P * c + P], xs_t[:, c, P * j:P * j + P], ident[:])
                ins.then_inc(xs_turned, 1)
            for s in range(8):
                g, j = divmod(s, NT)
                rows = slice(SSM_HD * g, SSM_HD * g + SSM_HD)
                if s < 4:
                    pe.wait_ge(xdt_done, s + 1)
                else:
                    pe.wait_ge(cb_done, s - 3)
                pe.matmul(bank[:, 4 + s % 4, 0:WIDTH[j]], xs_t[rows, 4, P * j:P * j + P], xs_t[rows, 5, P * j:TOK],
                          start=True, stop=True).then_inc(cb_ready, 1)
            pe.wait_ge(cb_done, 8)
            pe.wait_ge(rows_split, 2)
            for s in range(len(SSD_TASKS) + 2):
                if s < len(SSD_TASKS):
                    (h, j), b = SSD_TASKS[s], 4 + s % 2
                    w = WIDTH[j]
                    wait(pe, dec_done, s - 1)
                    if w > P:
                        pe.matmul(bank[:, b, P:w], head_row(h), a_rows[:, P * j + P:TOK], start=True, stop=True)
                    pe.matmul(bank[:, b, 0:P], head_row(h), a_rows[:, P * j:P * j + P], start=True, stop=False)
                    pe.matmul(bank[:, b, 0:P], ident_r[:], mask_st[:], start=False, stop=True).then_inc(dec_ready, 1)
                    if s % 2 == 0:
                        r = s // 2
                        feature_tile(n_sc + 1 + r // 8, (r // 4) % 2, ks=range(2 * (r % 4), 2 * (r % 4) + 2))
                if s >= 2:
                    h, j = SSD_TASKS[s - 2]
                    rows = slice(SSM_HD * (h % 2), SSM_HD * (h % 2) + SSM_HD)
                    pe.wait_ge(g_ready, s - 1)
                    if h % 2 == 0 and j == 0:
                        wait(pe, y_pair, h // 2 - 1)
                    pe.matmul(bank[rows, 6 + (h // 2) % 2, P * j:TOK], xdt[:, j, SSM_HD * h:SSM_HD * h + SSM_HD], g_ssd[:, s % 2, 0:WIDTH[j]],
                              start=(j == 0), stop=(j == NT - 1)).then_inc(ys_done, 1)
            def gate_unit(n, pace):
                for f in range(2):
                    feature_tile(n, f, pace)

            def branches(n, pace):
                u = UNITS[n]
                hi, lo = ktiles(w_hi[u["slot"]], 8, 256), ktiles(w_lo[u["slot"]], 8, 256)
                wait(pe, lo_done, n + 1 + pace.by(pace.units))
                for f in range(2):
                    fs = slice(P * f, P * f + P)
                    wait(pe, emptied[2 + f], u["round"] + pace.by(pace.rounds))
                    for b, k0, x_hi, x_lo, kt in ((4 + 2 * f, 2, sb_hi, sb_lo, 2), (5 + 2 * f, 4, ssm_hi, ssm_lo, 4), (2 + f, 0, sc_hi, sc_lo, 2)):
                        for k in range(kt):
                            ins = three_passes(bank[:, b, :], hi[:, k0 + k, fs], lo[:, k0 + k, fs], x_hi[:, k, :], x_lo[:, k, :],
                                               k == 0, k == kt - 1)
                    ins.then_inc(acc_full, 1)

            gate_unit(n_mg, STILL)
            pe.wait_ge(sq_done, 4)
            for g in range(2):
                for t in range(NT):
                    for c in (2 * g, 2 * g + 1):
                        q = NT * g + t
                        ins = pe.matmul(bank[:, 4, q:q + 1], z_t[:, c, P * t:P * t + P], ones[:, 0:1],
                                        start=(c % 2 == 0), stop=(c % 2 == 1))
            ins.then_inc(ss_ready, 1)
            gate_unit(n_mg + 1, STILL)
            pe.wait_ge(rr_diags, 1)
            for g in range(2):
                for t in range(NT):
                    ins = pe.matmul(bank[:, 4 + g, P * t:P * t + P], ones[:], rr_diag[:, NT * g + t, :], start=True, stop=True)
                ins.then_inc(rr_spread, 1)
            mod_columns(3)
            gate_unit(n_mg + 2, STILL)
            pe.wait_ge(sb_lo_done, 2)
            pe.wait_ge(sc_lo_done, 2)
            pe.wait_ge(ssm_lo_done, 4)
            pe.wait_ge(mod_out, 4)
            branches(n_mg + 3, STILL)
            with pe.Fori(0, 3) as p:
                for g in range(3):
                    gate_unit(n_mg + 4 + g, merge_pace(p))
                branches(n_mg + 7, merge_pace(p))
            for c in range(2):
                for j in range(2):
                    pe.wait_ge(m2_lo_done, 4 * j + 4)
                    token_unit(n_out2 + 2 * c + j, m2_hi, m2_lo, 4 * j, j == 0, j == 1, STILL)
                    if c == j == 0:
                        pe.wait_ge(m2_ready, KD)
                        mod_gate(4, 4)
            f_pairs(n_up2, KF // 2, c=3, xn=xn_2)
            mod_gate(5, 6)
            down(n_dn2, 1)


INPUTS = [
    "x", "mix_pre_g", "w_in", "b_forget", "sgu_norm_g", "w_spatial", "b_spatial", "w_out", "mix_post_g",
    "ffn_pre_g", "w_gate", "w_up", "w_down", "ffn_post_g", "c_2", "mod_w_2", "mod_b_2", "g_pre_mix_2",
    "g_post_mix_2", "g_pre_ffn_2", "g_post_ffn_2", "w_in_2", "sc_conv_w_2", "ssm_conv_w_2", "ssm_conv_b_2",
    "ssm_dt_bias_2", "ssm_a_log_2", "ssm_d_2", "ssm_norm_w_2", "w_sc_out_2", "w_sb_out_2", "w_ssm_out_2",
    "w_o_2", "w_ffn_in_2", "w_ffn_out_2",
]


def kernel(**inputs):
    import concourse.bacc as bacc
    from concourse.bass_utils import run_bass_kernel_spmd

    nc = bacc.Bacc("TRN2", target_bir_lowering=False, num_devices=1)
    arrays, args = {}, {}
    for name in INPUTS:
        array = np.ascontiguousarray(inputs[name])
        arrays[f"in_{name}"] = array
        args[name] = nc.dram_tensor(f"in_{name}", array.shape, mybir.dt.from_np(array.dtype), kind="ExternalInput").ap()
    out = nc.dram_tensor("out_0", arrays["in_x"].shape, F32, kind="ExternalOutput").ap()
    build(nc, args, out)
    result = run_bass_kernel_spmd(nc, [arrays], core_ids=[0])
    return result.results[0]["out_0"]
```
